# Optimizing a Trainium2 kernel written in Bass

```python
import math
import jax
import jax.numpy as jnp
from jax import lax
import numpy as np

D_MODEL = 1024
BATCH = 1
SEQ = 256
DEPTH = 2
DEC_BATCH = 8
DEC_SEQ = 1
PAST_LEN = 2048
PAGE_SIZE = 128

HEAD_DIM = 64
N_HEADS = D_MODEL // HEAD_DIM
ATTN_WIDTH = N_HEADS * HEAD_DIM
ATTN_SCALE = HEAD_DIM ** -0.5
D_FF = 4 * D_MODEL
RMS_EPS = 1e-6
REL_BUCKETS = 32
REL_MAX_DIST = 2048
DIL_PATTERNS = ((128, 1), (512, 4), (2048, 16))
N_DIL = len(DIL_PATTERNS)
A_Q_BLOCK = 64
A_IN_COLS = N_DIL * 3 * ATTN_WIDTH
NSA_KV_HEADS = 4
NSA_GROUP = N_HEADS // NSA_KV_HEADS
CMP_LEN = 32
CMP_STRIDE = 16
CMP_HIDDEN = 2 * HEAD_DIM
SEL_BLOCK = 64
SEL_TOPK = 16
SEL_FORCE = 1e4
SLIDE_WIN = 512
B_Q_BLOCK = 32
N_KV_BRANCH = 6
N_PAGED = 4
B_IN_COLS = ATTN_WIDTH + N_KV_BRANCH * NSA_KV_HEADS * HEAD_DIM + 3 * N_HEADS
N_LAYERS_A = (DEPTH + 1) // 2
N_LAYERS_B = DEPTH // 2

kernel_name = 'hybrid_dilated_nsa_decoder_step'

def rms_norm(x, g):
    xf = x.astype(jnp.float32)
    y = xf * lax.rsqrt(jnp.mean(xf * xf, axis=-1, keepdims=True) + RMS_EPS)
    return (y * g.astype(jnp.float32)).astype(x.dtype)

def rel_bucket(dist):
    dist = jnp.maximum(dist, 0)
    max_exact = REL_BUCKETS // 2
    ratio = jnp.log(jnp.maximum(dist, 1).astype(jnp.float32) / max_exact) / math.log(REL_MAX_DIST / max_exact)
    large = jnp.minimum(max_exact + (ratio * (REL_BUCKETS - max_exact)).astype(jnp.int32), REL_BUCKETS - 1)
    return jnp.where(dist < max_exact, dist, large)

def masked_softmax(logits, valid):
    logits = jnp.where(valid, logits.astype(jnp.float32), -jnp.inf)
    m = jnp.max(logits, axis=-1, keepdims=True)
    m = jnp.where(jnp.isfinite(m), m, 0.0)
    e = jnp.where(valid, jnp.exp(logits - m), 0.0)
    return e / jnp.maximum(jnp.sum(e, axis=-1, keepdims=True), 1e-30)

def squared_relu_mlp(h, w_up, w_down):
    return jnp.square(jax.nn.relu(h @ w_up)) @ w_down

def dilated_group(q, k, v, q_idx, window, dil, table):
    n_keys = window // dil + 1
    offs = dil * jnp.arange(n_keys, dtype=jnp.int32)
    idx = q_idx[:, None] - offs[None, :]
    valid = idx >= 0
    idx = jnp.maximum(idx, 0)
    kg = k[:, idx]
    vg = v[:, idx]
    bias = table.astype(jnp.float32)[rel_bucket(offs)].T
    logits = jnp.einsum('bqhd,bqjhd->bqhj', q, kg).astype(jnp.float32) * ATTN_SCALE + bias
    logits = jnp.where(valid[None, :, None, :], logits, -jnp.inf)
    m = jnp.max(logits, axis=-1, keepdims=True)
    e = jnp.exp(logits - m)
    s = jnp.sum(e, axis=-1, keepdims=True)
    o = jnp.einsum('bqhj,bqjhd->bqhd', (e / s).astype(v.dtype), vg)
    return o, m + jnp.log(s)

def merge_by_denominator(outs, lses):
    w = jax.nn.softmax(jnp.stack(lses), axis=0)
    return jnp.sum(w * jnp.stack(outs).astype(jnp.float32), axis=0)

def mixer_a_prompt(h, w_in, w_out, table):
    bsz, seq, _ = h.shape
    qkv = (h @ w_in).reshape(bsz, seq, N_DIL, 3, N_HEADS, HEAD_DIM)
    qs = [qkv[:, :, g, 0] for g in range(N_DIL)]
    ks = [qkv[:, :, g, 1] for g in range(N_DIL)]
    vs = [qkv[:, :, g, 2] for g in range(N_DIL)]

    def block(q0):
        q_idx = q0 + jnp.arange(A_Q_BLOCK, dtype=jnp.int32)
        outs, lses = [], []
        for g, (window, dil) in enumerate(DIL_PATTERNS):
            qb = lax.dynamic_slice_in_dim(qs[g], q0, A_Q_BLOCK, axis=1)
            o, l = dilated_group(qb, ks[g], vs[g], q_idx, window, dil, table)
            outs.append(o)
            lses.append(l)
        return merge_by_denominator(outs, lses)

    starts = jnp.arange(seq // A_Q_BLOCK, dtype=jnp.int32) * A_Q_BLOCK
    o = jnp.moveaxis(lax.map(block, starts), 0, 1).reshape(bsz, seq, ATTN_WIDTH)
    y = o.astype(h.dtype) @ w_out
    bufs = [qkv[:, seq - min(window, seq):, g, 1:3] for g, (window, _) in enumerate(DIL_PATTERNS)]
    return y, bufs

def mixer_a_sample(h, bufs, w_in, w_out, table):
    bsz, nt, _ = h.shape
    qkv = (h @ w_in).reshape(bsz, nt, N_DIL, 3, N_HEADS, HEAD_DIM)
    outs, lses, new_bufs = [], [], []
    for g, (window, dil) in enumerate(DIL_PATTERNS):
        buf_len = bufs[g].shape[1]
        past_len = PAST_LEN
        kv_all = jnp.concatenate([bufs[g], qkv[:, :, g, 1:3]], axis=1)
        q_idx = buf_len + jnp.arange(nt, dtype=jnp.int32)
        o, l = dilated_group(qkv[:, :, g, 0], kv_all[:, :, 0], kv_all[:, :, 1], q_idx, window, dil, table)
        outs.append(o)
        lses.append(l)
        keep = min(window, past_len + nt)
        new_bufs.append(kv_all[:, kv_all.shape[1] - keep:])
    o = merge_by_denominator(outs, lses).reshape(bsz, nt, ATTN_WIDTH)
    return o.astype(h.dtype) @ w_out, new_bufs

def split_b(proj, bsz, nt):
    n_kv = N_KV_BRANCH * NSA_KV_HEADS * HEAD_DIM
    q = proj[..., :ATTN_WIDTH].reshape(bsz, nt, N_HEADS, HEAD_DIM)
    kv = proj[..., ATTN_WIDTH:ATTN_WIDTH + n_kv].reshape(bsz, nt, N_KV_BRANCH, NSA_KV_HEADS, HEAD_DIM)
    gate = jax.nn.sigmoid(proj[..., ATTN_WIDTH + n_kv:].astype(jnp.float32)).reshape(bsz, nt, N_HEADS, 3)
    return q, kv, gate

def compress(rows, pe, w1, w2):
    bsz, t = rows.shape[:2]
    n = (t - CMP_LEN) // CMP_STRIDE + 1
    r = CMP_LEN // CMP_STRIDE
    chunks = rows[:, :CMP_STRIDE * (n + r - 1)].reshape(bsz, n + r - 1, CMP_STRIDE, NSA_KV_HEADS, HEAD_DIM)
    w1r = w1.reshape(r, CMP_STRIDE, HEAD_DIM, CMP_HIDDEN)
    pe_r = pe.reshape(r, CMP_STRIDE, HEAD_DIM)
    hid = None
    for i in range(r):
        part = jnp.einsum('bnsgd,sdh->bngh', chunks[:, i:i + n] + pe_r[i][:, None, :], w1r[i])
        hid = part if hid is None else hid + part
    return jnp.einsum('bngh,hd->bngd', jax.nn.relu(hid), w2)

def nsa_attend(q, gate, kc, vc, k_sel, v_sel, k_win, v_win, q_pos, win_start, table):
    bsz, nq = q.shape[:2]
    G, R = NSA_KV_HEADS, NSA_GROUP
    qg = q.reshape(bsz, nq, G, R, HEAD_DIM)
    tbl = table.astype(jnp.float32).reshape(REL_BUCKETS, G, R)

    n_cmp = kc.shape[1]
    c_end = jnp.arange(n_cmp, dtype=jnp.int32) * CMP_STRIDE + (CMP_LEN - 1)
    dist_c = q_pos[:, None] - c_end[None, :]
    bias_c = jnp.transpose(tbl[rel_bucket(dist_c)], (0, 2, 3, 1))
    logit_c = jnp.einsum('bqgrd,bngd->bqgrn', qg, kc).astype(jnp.float32) * ATTN_SCALE + bias_c[None]
    p_c = masked_softmax(logit_c, (dist_c >= 0)[None, :, None, None, :])
    o_c = jnp.einsum('bqgrn,bngd->bqgrd', p_c.astype(vc.dtype), vc)

    n_keys = k_sel.shape[1]
    n_blk = -(-n_keys // SEL_BLOCK)
    ratio = SEL_BLOCK // CMP_STRIDE
    span = CMP_LEN // CMP_STRIDE
    imp = jnp.pad(jnp.sum(p_c, axis=3), ((0, 0), (0, 0), (0, 0), (span - 1, ratio * n_blk - n_cmp)))
    imp_blk = jnp.zeros((bsz, nq, G, n_blk), jnp.float32)
    for m in range(ratio):
        for n in range(span):
            off = m - n + span - 1
            imp_blk = imp_blk + imp[..., off:off + ratio * n_blk:ratio]
    blk = jnp.arange(n_blk, dtype=jnp.int32)
    cur = q_pos // SEL_BLOCK
    forced = (blk[None, :] == 0) | (blk[None, :] == cur[:, None]) | (blk[None, :] == cur[:, None] - 1)
    causal_blk = blk[None, :] * SEL_BLOCK <= q_pos[:, None]
    score = jnp.where(forced[None, :, None, :], SEL_FORCE,
                      jnp.where(causal_blk[None, :, None, :], imp_blk, -1.0))
    n_top = min(SEL_TOPK, n_blk)
    _, sel = lax.top_k(score, n_top)
    pad = n_blk * SEL_BLOCK - n_keys

    def to_blocks(x):
        x = jnp.pad(x, ((0, 0), (0, pad), (0, 0), (0, 0)))
        return jnp.transpose(x.reshape(bsz, n_blk, SEL_BLOCK, G, HEAD_DIM), (0, 3, 1, 2, 4))

    sel_g = jnp.transpose(sel, (0, 2, 1, 3)).reshape(bsz, G, nq * n_top)
    bi = jnp.arange(bsz)[:, None, None]
    gi = jnp.arange(G)[None, :, None]
    ks_g = to_blocks(k_sel)[bi, gi, sel_g].reshape(bsz, G, nq, n_top * SEL_BLOCK, HEAD_DIM)
    vs_g = to_blocks(v_sel)[bi, gi, sel_g].reshape(bsz, G, nq, n_top * SEL_BLOCK, HEAD_DIM)
    pos_s = (sel[..., None] * SEL_BLOCK + jnp.arange(SEL_BLOCK, dtype=jnp.int32)).reshape(bsz, nq, G, n_top * SEL_BLOCK)
    dist_s = q_pos[None, :, None, None] - pos_s
    bias_s = jnp.moveaxis(tbl[rel_bucket(dist_s), jnp.arange(G)[None, None, :, None]], 4, 3)
    logit_s = jnp.einsum('bqgrd,bgqkd->bqgrk', qg, ks_g).astype(jnp.float32) * ATTN_SCALE + bias_s
    p_s = masked_softmax(logit_s, (dist_s >= 0)[:, :, :, None, :])
    o_s = jnp.einsum('bqgrk,bgqkd->bqgrd', p_s.astype(vs_g.dtype), vs_g)

    n_w = k_win.shape[1]
    w_pos = win_start + jnp.arange(n_w, dtype=jnp.int32)
    dist_w = q_pos[:, None] - w_pos[None, :]
    valid_w = (dist_w >= 0) & (dist_w < SLIDE_WIN) & (w_pos[None, :] >= 0)
    bias_w = jnp.transpose(tbl[rel_bucket(dist_w)], (0, 2, 3, 1))
    logit_w = jnp.einsum('bqgrd,bsgd->bqgrs', qg, k_win).astype(jnp.float32) * ATTN_SCALE + bias_w[None]
    p_w = masked_softmax(logit_w, valid_w[None, :, None, None, :])
    o_w = jnp.einsum('bqgrs,bsgd->bqgrd', p_w.astype(v_win.dtype), v_win)

    gate = gate.reshape(bsz, nq, G, R, 3).astype(q.dtype)
    o = gate[..., 0:1] * o_c + gate[..., 1:2] * o_s + gate[..., 2:3] * o_w
    return o.reshape(bsz, nq, ATTN_WIDTH)

def mixer_b_prompt(h, w_in, w_out, phi_pe, phi_w1, phi_w2, table):
    bsz, seq, _ = h.shape
    q, kv, gate = split_b(h @ w_in, bsz, seq)
    kc = compress(kv[:, :, 0], phi_pe[0], phi_w1[0], phi_w2[0])
    vc = compress(kv[:, :, 1], phi_pe[1], phi_w1[1], phi_w2[1])
    k_sel, v_sel = kv[:, :, 2], kv[:, :, 3]
    win_pad = jnp.pad(kv[:, :, N_PAGED:], ((0, 0), (SLIDE_WIN, 0), (0, 0), (0, 0), (0, 0)))

    def block(q0):
        qb = lax.dynamic_slice_in_dim(q, q0, B_Q_BLOCK, axis=1)
        gb = lax.dynamic_slice_in_dim(gate, q0, B_Q_BLOCK, axis=1)
        wb = lax.dynamic_slice_in_dim(win_pad, q0, SLIDE_WIN + B_Q_BLOCK, axis=1)
        q_pos = q0 + jnp.arange(B_Q_BLOCK, dtype=jnp.int32)
        return nsa_attend(qb, gb, kc, vc, k_sel, v_sel, wb[:, :, 0], wb[:, :, 1], q_pos, q0 - SLIDE_WIN, table)

    starts = jnp.arange(seq // B_Q_BLOCK, dtype=jnp.int32) * B_Q_BLOCK
    o = jnp.moveaxis(lax.map(block, starts), 0, 1).reshape(bsz, seq, ATTN_WIDTH)
    y = o.astype(h.dtype) @ w_out
    keep = min(SLIDE_WIN, seq)
    return y, kv[:, :, :N_PAGED], kv[:, seq - keep:, N_PAGED:]

def mixer_b_sample(h, cache_kv, cache_win, layer, page_table, w_in, w_out, phi_pe, phi_w1, phi_w2, table):
    bsz, nt, _ = h.shape
    q, kv, gate = split_b(h @ w_in, bsz, nt)
    past_len = page_table.shape[1] * cache_kv.shape[2]

    def rows(kind):
        past = cache_kv[layer, page_table, :, kind].reshape(bsz, past_len, NSA_KV_HEADS, HEAD_DIM)
        return jnp.concatenate([past, kv[:, :, kind]], axis=1)

    kc = compress(rows(0), phi_pe[0], phi_w1[0], phi_w2[0])
    vc = compress(rows(1), phi_pe[1], phi_w1[1], phi_w2[1])
    win_all = jnp.concatenate([cache_win[layer], kv[:, :, N_PAGED:]], axis=1)
    q_pos = past_len + jnp.arange(nt, dtype=jnp.int32)
    o = nsa_attend(q, gate, kc, vc, rows(2), rows(3), win_all[:, :, 0], win_all[:, :, 1],
                   q_pos, past_len - cache_win.shape[2], table)
    y = o.astype(h.dtype) @ w_out
    keep = min(SLIDE_WIN, past_len + nt)
    return y, kv[:, :, :N_PAGED], win_all[:, win_all.shape[1] - keep:]

def setup_inputs(seed: int = 0) -> dict:
    key = jax.random.key(seed)
    ks = jax.random.split(key, 24)
    n_pages = PAST_LEN // PAGE_SIZE
    n_used = DEC_BATCH * n_pages
    n_pool = n_used + max(1, n_used // 4)

    def nrm(k, shape, s):
        return jax.random.normal(k, shape, jnp.float32) * s

    inp = {}
    inp['x_prompt'] = nrm(ks[0], (BATCH, SEQ, D_MODEL), 1.0)
    inp['x_sample'] = nrm(ks[1], (DEC_BATCH, DEC_SEQ, D_MODEL), 1.0)
    for g, (window, _) in enumerate(DIL_PATTERNS):
        inp[f'cache_a_win{g}'] = nrm(ks[2 + g], (N_LAYERS_A, DEC_BATCH, min(window, PAST_LEN), 2, N_HEADS, HEAD_DIM), 1.0)
    inp['cache_b_kv'] = nrm(ks[5], (N_LAYERS_B, n_pool, PAGE_SIZE, N_PAGED, NSA_KV_HEADS, HEAD_DIM), 1.0)
    inp['cache_b_win'] = nrm(ks[6], (N_LAYERS_B, DEC_BATCH, min(SLIDE_WIN, PAST_LEN), 2, NSA_KV_HEADS, HEAD_DIM), 1.0)
    inp['page_table'] = jax.random.permutation(ks[7], n_pool)[:n_used].reshape(DEC_BATCH, n_pages).astype(jnp.int32)
    inp['rel_bias'] = nrm(ks[8], (REL_BUCKETS, N_HEADS), 0.5)
    inp['norm_mix'] = 1.0 + nrm(ks[9], (DEPTH, D_MODEL), 0.05)
    inp['norm_mlp'] = 1.0 + nrm(ks[10], (DEPTH, D_MODEL), 0.05)
    inp['norm_final'] = 1.0 + nrm(ks[11], (D_MODEL,), 0.05)
    inp['a_w_in'] = nrm(ks[12], (N_LAYERS_A, D_MODEL, A_IN_COLS), D_MODEL ** -0.5)
    inp['a_w_out'] = nrm(ks[13], (N_LAYERS_A, ATTN_WIDTH, D_MODEL), ATTN_WIDTH ** -0.5)
    inp['b_w_in'] = nrm(ks[14], (N_LAYERS_B, D_MODEL, B_IN_COLS), D_MODEL ** -0.5)
    inp['b_w_out'] = nrm(ks[15], (N_LAYERS_B, ATTN_WIDTH, D_MODEL), ATTN_WIDTH ** -0.5)
    inp['b_phi_pe'] = nrm(ks[16], (N_LAYERS_B, 2, CMP_LEN, HEAD_DIM), 0.5)
    inp['b_phi_w1'] = nrm(ks[17], (N_LAYERS_B, 2, CMP_LEN * HEAD_DIM, CMP_HIDDEN), (CMP_LEN * HEAD_DIM) ** -0.5)
    inp['b_phi_w2'] = nrm(ks[18], (N_LAYERS_B, 2, CMP_HIDDEN, HEAD_DIM), (CMP_HIDDEN / 2) ** -0.5)
    inp['mlp_w_up'] = nrm(ks[19], (DEPTH, D_MODEL, D_FF), D_MODEL ** -0.5)
    inp['mlp_w_down'] = nrm(ks[20], (DEPTH, D_FF, D_MODEL), D_FF ** -0.5)
    return inp

def reference(x_prompt, x_sample, cache_a_win0, cache_a_win1, cache_a_win2, cache_b_kv, cache_b_win,
              page_table, rel_bias, norm_mix, norm_mlp, norm_final, a_w_in, a_w_out, b_w_in, b_w_out,
              b_phi_pe, b_phi_w1, b_phi_w2, mlp_w_up, mlp_w_down):
    a_caches = (cache_a_win0, cache_a_win1, cache_a_win2)
    hp, hs = x_prompt, x_sample
    a_new_p = [[] for _ in range(N_DIL)]
    a_new_s = [[] for _ in range(N_DIL)]
    b_kv_p, b_kv_s, b_win_p, b_win_s = [], [], [], []
    for i in range(DEPTH):
        j = i // 2
        hn_p = rms_norm(hp, norm_mix[i])
        hn_s = rms_norm(hs, norm_mix[i])
        if i % 2 == 0:
            yp, bufs_p = mixer_a_prompt(hn_p, a_w_in[j], a_w_out[j], rel_bias)
            ys, bufs_s = mixer_a_sample(hn_s, [c[j] for c in a_caches], a_w_in[j], a_w_out[j], rel_bias)
            for g in range(N_DIL):
                a_new_p[g].append(bufs_p[g])
                a_new_s[g].append(bufs_s[g])
        else:
            yp, kvp, winp = mixer_b_prompt(hn_p, b_w_in[j], b_w_out[j], b_phi_pe[j], b_phi_w1[j], b_phi_w2[j], rel_bias)
            ys, kvs, wins = mixer_b_sample(hn_s, cache_b_kv, cache_b_win, j, page_table, b_w_in[j], b_w_out[j],
                                           b_phi_pe[j], b_phi_w1[j], b_phi_w2[j], rel_bias)
            b_kv_p.append(kvp)
            b_kv_s.append(kvs)
            b_win_p.append(winp)
            b_win_s.append(wins)
        hp = hp + yp
        hs = hs + ys
        hp = hp + squared_relu_mlp(rms_norm(hp, norm_mlp[i]), mlp_w_up[i], mlp_w_down[i])
        hs = hs + squared_relu_mlp(rms_norm(hs, norm_mlp[i]), mlp_w_up[i], mlp_w_down[i])
    y_prompt = rms_norm(hp, norm_final)
    y_sample = rms_norm(hs, norm_final)
    a_win0_prompt = jnp.stack(a_new_p[0])
    a_win0_sample = jnp.stack(a_new_s[0])
    a_win1_prompt = jnp.stack(a_new_p[1])
    a_win1_sample = jnp.stack(a_new_s[1])
    a_win2_prompt = jnp.stack(a_new_p[2])
    a_win2_sample = jnp.stack(a_new_s[2])
    b_kv_prompt = jnp.stack(b_kv_p)
    b_kv_sample = jnp.stack(b_kv_s)
    b_win_prompt = jnp.stack(b_win_p)
    b_win_sample = jnp.stack(b_win_s)
    return (y_prompt, y_sample, a_win0_prompt, a_win0_sample, a_win1_prompt, a_win1_sample,
            a_win2_prompt, a_win2_sample, b_kv_prompt, b_kv_sample, b_win_prompt, b_win_sample)


_drawn_inputs = setup_inputs


def setup_inputs(seed=0):
    import zlib

    import numpy as np

    out = dict(_drawn_inputs(seed))
    spreads = {}
    factors = {}
    for name, (base, spread) in spreads.items():
        noise = np.random.default_rng([zlib.crc32(name.encode()), seed]).standard_normal(out[name].shape)
        drawn = base * np.exp(spread * noise) if base else spread * noise
        out[name] = jnp.asarray(drawn.astype(out[name].dtype))
    for name, factor in factors.items():
        out[name] = (out[name] * factor).astype(out[name].dtype)
    return out
```

```python
from contextlib import ExitStack

import concourse.bass as bass
import numpy as np
from concourse import mybir

F32 = mybir.dt.float32
I32 = mybir.dt.int32
ALU = mybir.AluOpType
ACT = mybir.ActivationFunctionType
AX = mybir.AxisListType

P = 128
D = 1024
DC = D // P
SEQ = 256
RT = SEQ // P
NB = 8
R = SEQ + NB
H = 16
HD = 64
FF = 4 * D
FC = FF // P
SCALE = HD ** -0.5
EPS = 1e-6
NEG = -1e30
PAST = 2048
DIL = ((128, 1), (512, 4), (2048, 16))
NG = 3
KVH = 4
GW = KVH * HD
CMP = 15
CMPS = 127
NBLK = 33
TOPK = 16
WB = 256
NW = 4
NC = 2
SP_PAGES = 10
NT = 4

SL_A, SL_SEL, SL_WIN, SL_CMP, SL_NEW, NSL = 0, 3, 19, 23, 24, 25
NSL4 = -(-NSL // 4)

B_AIN, B_AOUT, B_UP0, B_DN0, B_BIN, B_BOUT, B_UP1, B_DN1, B_END = 0, 36, 40, 56, 72, 83, 87, 103, 119


def bucket(dist):
    d = np.maximum(dist, 0)
    ratio = np.log(np.maximum(d, 1).astype(np.float32) / 16) / np.float32(np.log(128.0))
    large = np.minimum(16 + (ratio * 16).astype(np.int32), 31)
    return np.where(d < 16, d, large)


def onehot(dist):
    return (bucket(dist)[None, :] == np.arange(32)[:, None]).astype(np.float32)


def constants():
    p = np.arange(P)
    c = {"c_ident": np.eye(P, dtype=np.float32)}
    slots = [dil * (P - p) for _, dil in DIL]
    slots += [PAST - (16 * p + s) for s in range(16)]
    slots += [512 - (4 * p + s) for s in range(4)]
    slots += [PAST - (16 * p + 31), 0 * p]
    near = np.arange(-255, 256)
    slots += [0 * p] * (4 * NSL4 - len(slots))
    by4 = [np.concatenate([slots[4 * j + i] for j in range(NSL4)]) for i in range(4)]
    c["c_oh"] = np.concatenate([np.concatenate([onehot(near - i), onehot(near - 16 * i), onehot(by4[i])], 1) for i in range(4)])
    ms = np.zeros((P, NSL), np.float32)
    ms[0, SL_WIN] = NEG
    ms[P - 1, SL_CMP] = NEG
    c["c_mslot"] = ms
    q, kk = p[:, None], np.arange(2 * P)[None, :]
    dist = P + q - kk
    m = [(dist >= 0) & (dist % dil == 0) & (dist <= w) for w, dil in DIL] + [dist >= 0]
    c["c_mprompt"] = np.where(np.stack(m, 1), 0, NEG).astype(np.float32).reshape(P, 4 * 2 * P)
    dc = np.arange(RT)[None, :, None] * P + p[:, None, None] - 31 - 16 * np.arange(CMP)[None, None, :]
    c["c_mcmp"] = np.where(dc >= 0, 0, NEG).astype(np.float32).reshape(P, RT * CMP)
    c["c_mnew"] = np.where(np.eye(NB) > 0, 0, NEG).astype(np.float32)
    imp = np.zeros((P, NBLK), np.float32)
    for j in range(NBLK):
        for m_ in range(4):
            for n_ in range(2):
                i = 4 * j + m_ - n_
                if 0 <= i < CMPS:
                    imp[i, j] += 1
    c["c_imp"] = imp
    e = np.zeros((NBLK, P), np.float32)
    e[p // 4, p] = 1
    c["c_blk"] = e
    j, i = np.arange(NBLK)[:, None], np.arange(NBLK)[None, :]
    c["c_before"] = np.broadcast_to((i < j).astype(np.float32), (4 * NB, NBLK, NBLK)).reshape(4 * NB, NBLK * NBLK).copy()
    return c


SEMS = """table_zero consts_in x_loaded ones_ready gemm_done gemm_evac gains_turned gains_ready bias_done bias_evac
sq_ready sumsq_done var_ready std_ready h_ready rows_turned rows_evac rows_stored dve_own act_own pool_own
scores_done logits_read mix_ready max_ready probs_ready probs_turned pt_ready pv_done o_evac ot_turned ot_evac
qbd_ready newlog_done newlog_read sq_turned sq_evac_d sq_evac_a sq_used qk_done qk_read
smax_in smax_turned smax_diag smax_bc smax_sub smax_exp smax_sum smax_den smax_norm
pva_done pnew_done oa_ready up_ready w1_in pe_turned pe_ready peb_done peb_ready hid_ready comp_done comp_read acc_done
gate_raw gate_ready gate_turned gate_diag gateb_done gates_ready qb_ready
hidp_done hidp_ready kcp_done kcp_ready imp_ready score_done rank_ready rank_turned rankt_ready
selm_done selm_ready pvs_done pvw_done pvc_done ob_ready y_turned y_evac y_stored copies_done new_stored""".split()


def program(nc, t):
    with ExitStack() as ctx:
        def sb(name, shape, dt=F32):
            return ctx.enter_context(nc.sbuf_tensor(name, shape, dt))

        S = {n: ctx.enter_context(nc.semaphore(n)) for n in SEMS}
        w_landed = [ctx.enter_context(nc.semaphore(f"w_landed{i}")) for i in range(NW)]
        c_landed = [ctx.enter_context(nc.semaphore(f"c_landed{i}")) for i in range(NC)]
        p_landed = [ctx.enter_context(nc.semaphore(f"p_landed{i}")) for i in range(NC)]
        bk = [ctx.enter_context(nc.psum_tensor(f"bank{i}", [P, 512], F32)) for i in range(8)]

        xT = sb("xT", [P, DC, R])
        hT = sb("hT", [P, DC, R])
        oT = sb("oT", [P, DC, R])
        wring = sb("wring", [P, NW, DC, WB])
        cring = sb("cring", [P, NC, 4096])
        turned = sb("turned", [P, NT, 512])
        ident = sb("ident", [P, P])
        ones = sb("ones", [P, P])
        bias = sb("bias", [P, H, 2 * P])
        bias_s = sb("bias_s", [P, NSL, H])
        bias_c = sb("bias_c", [P, RT, H, CMP])
        mprompt = sb("mprompt", [P, 4, 2 * P])
        mslot = sb("mslot", [P, NSL])
        mcmp = sb("mcmp", [P, RT, CMP])
        mnew = sb("mnew", [NB, NB])
        imp_w = sb("imp_w", [P, NBLK])
        blk_e = sb("blk_e", [NBLK, P])
        pages = sb("pages", [1, P], I32)
        gains = sb("gains", [P, 40])
        nbias = sb("nbias", [NB, NB, H])
        rv = sb("rv", [P, 3, R])
        small = sb("small", [P, 512])
        AREA = 20336
        area = sb("area", [P, AREA])
        top = [0]

        def at(n, off=None, parts=P):
            o = top[0] if off is None else off
            if off is None:
                top[0] += n
            assert o + n <= AREA, (o + n)
            return area[0:parts, o:o + n]

        qT = at(NG * DC * R).rearrange("p (g c r) -> p g c r", g=NG, c=DC)
        kT = at(NG * DC * R).rearrange("p (g c r) -> p g c r", g=NG, c=DC)
        v_off = top[0]
        V = at(RT * NG * D).rearrange("p (t g n) -> p t g n", t=RT, g=NG)
        vTn = at(NG * DC * NB).rearrange("p (g c b) -> p g c b", g=NG, c=DC)
        qbd = at(NG * NB * H).rearrange("p (g b c e) -> p g b c e", g=NG, b=NB, e=2)
        mixes = (at(768), cring[:, 0, NG * D:NG * D + 768])
        turned_f = turned.rearrange("p i n -> p (i n)")
        oT_f = oT.rearrange("p c r -> p (c r)")
        krow = turned_f[:, 0:RT * D].rearrange("p (t n) -> p t n", t=RT)
        rown = oT_f[0:NB, 0:D]
        vtmp = oT_f[:, D:D + 2 * R].rearrange("p (i r) -> p i r", i=2)
        LG = turned_f[:, 0:2 * 768].rearrange("p (i n) -> p i n", i=2)
        PT = oT_f[:, 0:2 * 768].rearrange("p (i n) -> p i n", i=2)
        top[0] = v_off
        LA = at(NB * 6 * H).rearrange("p (b s h) -> p b s h", b=NB, s=6)
        pn = at(NB * NG * H).rearrange("p (b g c e) -> p b g c e", b=NB, g=NG, e=2)
        pv3 = at(NG * NB * DC).rearrange("p (g b c) -> p g b c", g=NG, b=NB)
        pv1 = at(NB * DC).rearrange("p (b c) -> p b c", b=NB)
        orow = hT.rearrange("p c r -> p (c r)")[:, 0:RT * D].rearrange("p (t n) -> p t n", t=RT)
        NOH = 2 * 511 + NSL4 * P
        oh = cring[:, 1, 0:NOH]
        table = cring[:, 1, NOH:NOH + 4 * H]
        grow_ = cring[0:40, 1, NOH + 4 * H:NOH + 4 * H + P]
        xrow = at(RT * D, v_off).rearrange("p (t n) -> p t n", t=RT)
        xsrow = at(D, v_off + RT * D, parts=NB)
        upT = at(FC * R, 0)
        top[0] = 0
        qT2 = at(DC * R).rearrange("p (c r) -> p c r", c=DC)
        kvrow = at(RT * 6 * GW).rearrange("p (t n) -> p t n", t=RT)
        kvnew = at(6 * GW, parts=NB)
        kD = at(2 * KVH * SEQ).rearrange("p (k g t) -> p k g t", k=2, g=KVH)
        kcS = at(NB * 508, parts=HD).rearrange("p (b n) -> p b n", b=NB)
        vcS = at(NB * GW).rearrange("p (b n) -> p b n", b=NB)
        w2 = at(2 * HD).rearrange("p (k d) -> p k d", k=2)
        peT = at(32)
        peb = at(2)
        kcP = at(60)
        vcP = at(GW)
        gB = at(384).rearrange("p (h k b) -> p h k b", h=H, k=3)
        kTn = at(2 * 2 * NB).rearrange("p (k g b) -> p k g b", k=2, g=2)
        grow = at(RT * 48).rearrange("p (t h k) -> p t h k", t=RT, k=3)
        q0 = at(NB * H, parts=HD).rearrange("p (b h) -> p b h", b=NB)
        qb2 = at(NB * H).rearrange("p (b h) -> p b h", b=NB)
        selm = at(NB * KVH).rearrange("p (b g) -> p b g", b=NB)
        w1_off = top[0]
        w1 = at(2 * 2 * 8 * P).rearrange("p (k i s n) -> p k i s n", k=2, i=2, s=8)
        top[0] = w1_off
        LS = at(NB * 17 * H).rearrange("p (b s h) -> p b s h", b=NB, s=17)
        LSW = at(NB * 5 * H).rearrange("p (b s h) -> p b s h", b=NB, s=5)
        LC = at(NB * H).rearrange("p (b s h) -> p b s h", b=NB, s=1)
        kvtmp = oT_f[:, 0:2 * R].rearrange("p (i r) -> p i r", i=2)
        gdiag = oT_f[0:48, 0:384]
        gT = oT_f[:, 2 * R:3 * R]
        hid = oT_f[:, 1000:1000 + 2 * 508].rearrange("p (k n) -> p k n", k=2)
        PB = oT_f[:, 0:2 * 640].rearrange("p (i n) -> p i n", i=2)
        XTp = turned_f[:, 0:1024].rearrange("p (k s g n) -> p k s g n", k=2, s=8, g=KVH)
        LB = turned_f[:, 0:2 * 528].rearrange("p (i n) -> p i n", i=2)
        pe_row = small[0:32, 384:512]
        hidp = small[:, 128:128 + 2 * 60].rearrange("p (k n) -> p k n", k=2)
        rk = [at(NBLK * NBLK, i * NBLK * NBLK, parts=32).rearrange("p (j i) -> p j i", j=NBLK) for i in range(3)]
        before = at(NBLK * NBLK, 3 * NBLK * NBLK, parts=32).rearrange("p (j i) -> p j i", j=NBLK)
        score = at(NBLK, 4 * NBLK * NBLK, parts=32)
        rank = at(NBLK, 4 * NBLK * NBLK + NBLK, parts=32)
        rankT = at(32, 4 * NBLK * NBLK + 2 * NBLK, parts=NBLK)
        impb = at(32, 4 * NBLK * NBLK + 2 * NBLK + 32)
        ob = at(3 * P, 4 * NBLK * NBLK + 200).rearrange("p (k n) -> p k n", k=3)
        assert 4 * NBLK * NBLK + 700 <= DC * R + RT * 6 * GW
        mx2 = small[:, 0:12]
        sm2 = small[:, 12:24]
        rc2 = small[:, 24:36]
        m1 = small[:, 40:41]
        ob3 = small[:, 128:128 + 3 * HD].rearrange("p (k d) -> p k d", k=3)
        diag = small[:, 128:256]
        mxa = small[:, 256:384]
        rs = rv.rearrange("p k r -> p (k r)")[:, 0:3 * P].rearrange("p (k n) -> p k n", k=3)

        up_all = upT

        items = ([("ak", b) for b in range(NB)] + [("av", b) for b in range(NB)] +
                 [("cmp", b, x) for b in range(NB) for x in range(2)] +
                 [("sk", b) for b in range(NB)] + [("wk", b) for b in range(NB)] +
                 [("sv", b) for b in range(NB)] + [("wv", b) for b in range(NB)])
        n_dmas = {"ak": 3, "av": 3, "cmp": 16, "sk": 16, "wk": 1, "sv": 16, "wv": 1}
        index = {it: i for i, it in enumerate(items)}
        landed, tot = [], [[0, 0] for _ in range(NC)]
        for i, it in enumerate(items):
            n_sp = SP_PAGES if n_dmas[it[0]] == 16 else 0
            tot[i % NC][0] += 16 * (n_dmas[it[0]] - n_sp)
            tot[i % NC][1] += 16 * n_sp
            landed.append(tuple(tot[i % NC]))

        def arrived(eng, it):
            i = index[it]
            eng.wait_ge(c_landed[i % NC], landed[i][0])
            if landed[i][1]:
                eng.wait_ge(p_landed[i % NC], landed[i][1])

        def slot_of(it):
            return cring[:, index[it] % NC, :]

        groups = []
        for b in range(NB):
            for g in range(NG):
                for x in range(2):
                    src = slot_of(("ak", b))
                    groups.append((("ak", b), [src[:, g * D + (4 * x + i) * P:g * D + (4 * x + i + 1) * P] for i in range(4)],
                                   (g, x)))
        n_cmp0 = len(groups)
        for b in range(NB):
            for x in range(2):
                src = slot_of(("cmp", b, x)).rearrange("p (s k n) -> p s k n", s=8, k=2)
                for s in range(4):
                    for k in range(2):
                        groups.append((("cmp", b, x), [src[:, 2 * s + i // 2, k, (i % 2) * P:(i % 2 + 1) * P] for i in range(4)], (k, 4 * x + s)))
        n_sel0 = len(groups)
        for kind, ns in (("sk", 16), ("wk", 4)):
            for b in range(NB):
                src = slot_of((kind, b))
                for s in range(0, ns, 2):
                    groups.append(((kind, b), [src[:, (s + i // 2) * GW + (i % 2) * P:(s + i // 2) * GW + (i % 2 + 1) * P]
                                               for i in range(4)], (s,)))
        n_groups = len(groups)
        last_group = {}
        for n, gr in enumerate(groups):
            last_group[gr[0]] = n

        def copy_squares(copy, n):
            dst, src = turned[:, n % NT, :], bk[2 + n % 2]
            if not n_cmp0 <= n < n_sel0:
                return copy(dst, src[:, :])
            for y in range(2):
                for x in range(2):
                    ins = copy(dst[64 * y:64 * y + 64].rearrange("p (g x n) -> p g x n", g=2, x=2)[:, :, x, :],
                               src[64 * x:64 * x + 64, y * 256:(y + 1) * 256].rearrange("p (g n) -> p g n", g=2))
            return ins

        def freed(eng, i):
            it = items[i]
            if it in last_group:
                eng.wait_ge(S["sq_turned"], last_group[it] + 1)
            elif it[0] == "av":
                eng.wait_ge(S["pva_done"], it[1] + 1)
            elif it[0] == "sv":
                eng.wait_ge(S["pvs_done"], it[1] + 1)
            else:
                eng.wait_ge(S["pvw_done"], it[1] + 1)

        E_X, E_AIN, E_AOUT, E_UP0, E_DN0 = 0, 8, 80, 88, 120
        E_BIN, E_BOUT, E_UP1, E_DN1, E_ALL = 128, 149, 157, 189, 197

        def done_at(blk):
            return 8 + 2 * blk

        def page_loads(eng, i, js, landed_sem):
            it = items[i]
            kind, b = it[0], it[1]
            for j in js:
                page = eng.value_load(pages[0:1, b * 16 + j:b * 16 + j + 1], min_val=0, max_val=t["cache_b_kv"].shape[1] - 1)
                src = t["cache_b_kv"][0, bass.ds(page, 1)].rearrange("o (p s) k h d -> (o p) s k (h d)", s=16)
                if kind == "cmp":
                    src = src[:, 8 * it[2]:8 * it[2] + 8, 0:2, :].rearrange("p s k n -> p s (k n)")
                else:
                    src = src[:, :, 2 if kind == "sk" else 3, :]
                dst = cring[8 * j:8 * j + 8, i % NC, :].rearrange("p (s n) -> p s n", s=src.shape[1])
                eng.dma_start(dst, src).then_inc(landed_sem[i % NC], 16)

        block = ctx.enter_context(nc.Block())

        @block.sync
        def _(sp):
            sp.dma_start(xrow, t["x_prompt"].rearrange("a (t p) n -> p (a t) n", p=P)).then_inc(S["x_loaded"], 16)
            sp.dma_start(xsrow, t["x_sample"].rearrange("b a n -> (b a) n")).then_inc(S["x_loaded"], 16)
            for dst, src in ((ident[:, :], t["c_ident"]), (oh, t["c_oh"]),
                             (grow_[0:16], t["norm_mix"].rearrange("l (c n) -> (l c) n", n=P)),
                             (grow_[16:32], t["norm_mlp"].rearrange("l (c n) -> (l c) n", n=P)),
                             (grow_[32:40], t["norm_final"].rearrange("(c n) -> c n", n=P)),
                             (mprompt.rearrange("p m k -> p (m k)"), t["c_mprompt"]),
                             (mslot[:, :], t["c_mslot"]), (mcmp.rearrange("p t k -> p (t k)"), t["c_mcmp"]),
                             (mnew[:, :], t["c_mnew"]), (imp_w[:, :], t["c_imp"]), (blk_e[:, :], t["c_blk"])):
                sp.dma_start(dst, src).then_inc(S["consts_in"], 16)
            sp.wait_ge(S["table_zero"], 1)
            for i in range(4):
                sp.dma_start(table[32 * i:32 * i + 32, i * H:(i + 1) * H], t["rel_bias"]).then_inc(S["consts_in"], 16)

            shifts = []

            def shift(src, dst, parts, run):
                for b in range(NB):
                    s = src[0, b, 1:].rearrange("w a h d -> (w a h d)").rearrange("(n x m) -> n x m", n=parts, m=run)
                    d = dst[0, b, :dst.shape[2] - 1].rearrange("w a h d -> (w a h d)").rearrange("(n x m) -> n x m", n=parts, m=run)
                    for i in range(parts):
                        shifts.append((d[i], s[i]))
            shift(t["cache_a_win2"], t["a_win2_sample"], 8, 4094)
            shift(t["cache_a_win1"], t["a_win1_sample"], 2, 4088)
            shift(t["cache_a_win0"], t["a_win0_sample"], 1, 4064)
            shift(t["cache_b_win"], t["b_win_sample"], 1, 4088)

            def w_block(i):
                k = [x for x in (B_AIN, B_AOUT, B_UP0, B_DN0, B_BIN, B_BOUT, B_UP1, B_DN1) if x <= i][-1]
                j = i - k
                if k in (B_DN0, B_DN1):
                    w = t["mlp_w_down"][0 if k == B_DN0 else 1]
                    rows, j = (j % 4) * D, j // 4
                    return w[rows:rows + D].rearrange("(c p) n -> p c n", p=P)[:, :, j * WB:(j + 1) * WB]
                w = {B_AIN: t["a_w_in"][0], B_AOUT: t["a_w_out"][0], B_UP0: t["mlp_w_up"][0],
                     B_BIN: t["b_w_in"][0], B_BOUT: t["b_w_out"][0], B_UP1: t["mlp_w_up"][1]}[k]
                return w.rearrange("(c p) n -> p c n", p=P)[:, :, j * WB:min((j + 1) * WB, w.shape[1])]

            use = ([("w", i) for i in range(B_AOUT)] + [("c", i) for i in range(2 * NB)] +
                   [("w", i) for i in range(B_AOUT, B_BIN)] + [("c", i) for i in range(2 * NB, 4 * NB)] +
                   [("w", i) for i in range(B_BIN, B_BOUT)] + [("c", i) for i in range(4 * NB, 8 * NB)] +
                   [("w", i) for i in range(B_BOUT, B_END)])
            pos = {x: n for n, x in enumerate(use)}
            depth = {"w": NW, "c": NC}
            loads = sorted(use, key=lambda x: (pos.get((x[0], x[1] - depth[x[0]]), -1), pos[x]))
            for what, i in loads:
                if what == "c":
                    if n_dmas[items[i][0]] == 16:
                        if i == 2 * NB:
                            sp.wait_ge(S["pool_own"], 16)
                        freed(sp, i - NC)
                        page_loads(sp, i, range(SP_PAGES), p_landed)
                    continue
                if i >= NW:
                    sp.wait_ge(S["gemm_done"], done_at(i - NW + 1))
                src = w_block(i)
                sp.dma_start(wring[:, i % NW, :, 0:src.shape[2]], src).then_inc(w_landed[i % NW], 16)
                if i >= 4 and shifts:
                    d, s = shifts.pop(0)
                    sp.dma_start(d, s).then_inc(S["copies_done"], 16)
            while shifts:
                d, s = shifts.pop(0)
                sp.dma_start(d, s).then_inc(S["copies_done"], 16)
            n_shift = 8 * (8 + 2 + 1 + 1)
            sp.wait_ge(S["copies_done"], 16 * n_shift)

        @block.gpsimd
        def _(pool):
            nc.gpsimd.memset(ones[:, :], 1.0).then_inc(S["ones_ready"], 1)
            nc.gpsimd.memset(table, 0.0).then_inc(S["table_zero"], 1)

            def load(i):
                it = items[i]
                if i >= NC:
                    freed(pool, i - NC)
                if i == 1:
                    pool.wait_ge(S["bias_done"], 10)
                    pool.wait_ge(S["gains_turned"], 1)
                dst, sem = cring[:, i % NC, :], c_landed[i % NC]
                kind, b = it[0], it[1]
                if kind in ("ak", "av"):
                    for g, (w, dil) in enumerate(DIL):
                        src = t[f"cache_a_win{g}"][0, b].rearrange("(p r) a h d -> p r a (h d)", r=dil)
                        pool.dma_start(dst[:, g * D:(g + 1) * D], src[:, 0, 0 if kind == "ak" else 1, :]).then_inc(sem, 16)
                elif kind in ("wk", "wv"):
                    src = t["cache_b_win"][0, b].rearrange("(p r) a h d -> p r a (h d)", r=4)
                    pool.dma_start(dst[:, 0:4 * GW].rearrange("p (r n) -> p r n", r=4), src[:, :, 0 if kind == "wk" else 1, :]).then_inc(sem, 16)
                else:
                    page_loads(pool, i, range(SP_PAGES, 16), c_landed)

            pool.dma_start(pages[:, :], t["page_table"].rearrange("b n -> (b n)").unsqueeze(0)).then_inc(S["pool_own"], 16)
            load(0)
            load(1)
            pool.wait_ge(S["bias_evac"], 10)
            pool.wait_ge(S["rows_stored"], 16 * 12)
            for h in range(H):
                if h >= 2:
                    pool.wait_ge(S["logits_read"], 2 * h - 2)
                nc.gpsimd.tensor_tensor(mixes[h % 2].rearrange("p (g k) -> p g k", g=NG), bias[:, h, :].unsqueeze(1).broadcast_to([P, NG, 2 * P]),
                                        mprompt[:, 0:NG, :], ALU.add).then_inc(S["mix_ready"], 1)
            pool.wait_ge(S["mix_ready"], H)
            nc.gpsimd.tensor_tensor(bias[:, :, :], bias[:, :, :], mprompt[:, 3, :].unsqueeze(1).broadcast_to([P, H, 2 * P]), ALU.add)\
              .then_inc(S["mix_ready"], 1)
            pool.wait_ge(S["pool_own"], 16)
            for i in range(2, len(items)):
                load(i)

        @block.tensor
        def _(pe):
            pe.wait_ge(S["consts_in"], 16 * 15)
            pe.wait_ge(S["x_loaded"], 32)
            for c in range(DC):
                if c >= 2:
                    pe.wait_ge(S["gemm_evac"], c - 1)
                g = bk[c % 2]
                for rt in range(RT):
                    pe.transpose(g[:, rt * P:(rt + 1) * P], xrow[:, rt, c * P:(c + 1) * P], ident[:, :])
                pe.transpose(g[:, SEQ:R], xsrow[:, c * P:(c + 1) * P], ident[0:NB, 0:NB]).then_inc(S["gemm_done"], 1)
            pe.transpose(bk[2][:, 0:40], grow_, ident[0:40, 0:40]).then_inc(S["gains_turned"], 1)

            def norm(n):
                if n == 0:
                    pe.wait_ge(S["ones_ready"], 1)
                for c in range(DC):
                    pe.wait_ge(S["sq_ready"], DC * n + c + 1)
                    mm = pe.matmul(bk[7][:, 0:R], ones[:, :], oT[:, c, :], start=(c == 0), stop=(c == DC - 1))
                mm.then_inc(S["sumsq_done"], 1)

            norm(0)
            for i in range(8):
                if i >= 2:
                    pe.wait_ge(S["bias_evac"], i - 1)
                for k in range(0, 32, 4):
                    o = P - (32 * i + k) + 255
                    mm = pe.matmul(bk[3 + i % 2][:, k * H:(k + 4) * H], oh[:, o:o + P], table, start=True, stop=True)
                mm.then_inc(S["bias_done"], 1)
            for s in range(NSL4):
                mm = pe.matmul(bk[5][:, 4 * s * H:4 * (s + 1) * H], oh[:, 1022 + s * P:1022 + (s + 1) * P], table, start=True, stop=True)
            mm.then_inc(S["bias_done"], 1)
            for rt in range(RT):
                for n in range(0, 16, 4):
                    o, m = 511 + rt * P - 31 - 16 * n + 255, min(4, CMP - n)
                    mm = pe.matmul(bk[6][:, (rt * CMP + n) * H:(rt * CMP + n + m) * H], oh[:, o:o + P], table[:, 0:m * H], start=True, stop=True)
            mm.then_inc(S["bias_done"], 1)

            def rows(r, src):
                b = bk[2 + r % 2]
                if r >= 2:
                    pe.wait_ge(S["rows_evac"], r - 1)
                for rt in range(RT):
                    pe.transpose(b[:, rt * P:(rt + 1) * P], src[:, rt * P:(rt + 1) * P], ident[:, :])
                pe.transpose(b[0:NB, SEQ:SEQ + P], src[:, SEQ:R], ident[:, :]).then_inc(S["rows_turned"], 1)

            def tile(blk, half, e, rhs, width=P):
                pe.wait_ge(S["gemm_evac"], e - 1)
                for c in range(DC):
                    mm = pe.matmul(bk[half][0:width, 0:R], wring[:, blk % NW, c, half * P:half * P + width], rhs[:, c, :],
                                   start=(c == 0), stop=(c == DC - 1))
                return mm

            pe.wait_ge(S["h_ready"], DC)
            pe.wait_ge(S["bias_evac"], 8)
            pe.wait_ge(S["gains_ready"], 1)
            r, held = 0, None
            for blk in range(36):
                pe.wait_ge(w_landed[blk % NW], 16 * (blk // NW + 1))
                for half in range(2):
                    i = 2 * blk + half
                    tile(blk, half, E_AIN + i, hT).then_inc(S["gemm_done"], 1)
                    if held is not None:
                        pe.wait_ge(S["gemm_evac"], E_AIN + held[0] + 1)
                        rows(r, held[1])
                        r += 1
                    g, kind, c = i // 24, i // 8 % 3, i % 8
                    held = None if kind == 0 else (i, kT[:, g, c, :] if kind == 1 else vtmp[:, i % 2, :])
            pe.wait_ge(S["gemm_evac"], E_AOUT)
            rows(r, held[1])

            def score_a(u):
                h, qt = u // 2, u % 2
                q0, c = HD * (h % 2), h // 2
                if u >= 2:
                    pe.wait_ge(S["logits_read"], u - 1)
                n = (qt + 1) * P
                for g in range(NG):
                    out = bk[0][:, g * P:(g + 1) * P] if qt == 0 else (bk[1][:, g * 256:(g + 1) * 256] if g < 2 else bk[2][:, 0:256])
                    mm = pe.matmul(out, qT[q0:q0 + HD, g, c, qt * P:(qt + 1) * P], kT[q0:q0 + HD, g, c, 0:n], start=True, stop=True)
                mm.then_inc(S["scores_done"], 1)

            def turn_probs(u, widths, src):
                if u[1] >= 2:
                    pe.wait_ge(S["pt_ready"], u[0] - 1)
                pe.wait_ge(S["probs_ready"], u[0] + 1)
                at_ = 0
                for j, w in enumerate(widths):
                    b = bk[3] if u[1] % 2 == 0 else bk[4 + j // 4]
                    mm = pe.transpose(b[0:w, (j % 4) * P:(j % 4 + 1) * P], src[:, at_:at_ + w], ident[:, :])
                    at_ += w
                mm.then_inc(S["probs_turned"], 1)

            def pv_a(u):
                h, qt = u // 2, u % 2
                pe.wait_ge(S["pt_ready"], u + 1)
                if u >= 2:
                    pe.wait_ge(S["o_evac"], u - 1)
                n = qt + 1
                for j in range(NG * n):
                    mm = pe.matmul(bk[6 + u % 2][:, 0:HD], PT[:, u % 2, j * P:(j + 1) * P], V[:, j % n, j // n, h * HD:(h + 1) * HD],
                                   start=(j == 0), stop=(j == NG * n - 1))
                mm.then_inc(S["pv_done"], 1)

            pe.wait_ge(S["rows_evac"], 48)
            pe.wait_ge(S["bias_evac"], 10)
            score_a(0)
            for u in range(2 * H):
                if u + 1 < 2 * H:
                    score_a(u + 1)
                turn_probs((u, u), [P] * (NG * (u % 2 + 1)), LG[:, u % 2, :])
                if u:
                    pv_a(u - 1)
            pv_a(2 * H - 1)

            def turn_out(first):
                for c in range(DC):
                    if c >= 2 or first:
                        pe.wait_ge(S["ot_evac"], first + c - 1)
                    for rt in range(RT):
                        mm = pe.transpose(bk[c % 2][:, rt * P:(rt + 1) * P], orow[:, rt, c * P:(c + 1) * P], ident[:, :])
                    mm.then_inc(S["ot_turned"], 1)

            pe.wait_ge(S["o_evac"], 2 * H)
            turn_out(0)

            def turn(n):
                if n >= 2:
                    pe.wait_ge(S["sq_evac_d"] if n % 2 == 0 else S["sq_evac_a"], n // 2)
                it, src, _ = groups[n]
                arrived(pe, it)
                for i in range(4):
                    mm = pe.transpose(bk[2 + n % 2][:, i * P:(i + 1) * P], src[i], ident[:, :])
                mm.then_inc(S["sq_turned"], 1)

            def squares(n):
                pe.wait_ge(S["sq_evac_d"] if n % 2 == 0 else S["sq_evac_a"], n // 2 + 1)
                return turned[:, n % NT, :]

            pe.wait_ge(S["pt_ready"], 2 * H)
            pe.wait_ge(S["qbd_ready"], 2)
            for g in range(NG):
                for c in range(DC):
                    mm = pe.matmul(bk[6][0:NB, (g * DC + c) * 16:(g * DC + c + 1) * 16], kT[:, g, c, SEQ:R], qbd[:, g, :, c, :],
                                   start=True, stop=True)
            mm.then_inc(S["newlog_done"], 1)
            turn(0)
            for n in range(n_cmp0):
                if n + 1 < n_cmp0:
                    turn(n + 1)
                it, _, (g, x) = groups[n]
                b, sq = it[1], squares(n)
                if g == 0 and x == 0 and b >= 2:
                    pe.wait_ge(S["qk_read"], b - 1)
                for i in range(4):
                    c = 4 * x + i
                    mm = pe.matmul(bk[4 + b % 2][:, g * H + 2 * c:g * H + 2 * c + 2], sq[:, i * P:(i + 1) * P], qbd[:, g, b, c, :],
                                   start=True, stop=True)
                mm.then_inc(S["sq_used"], 1)

            def softmax(k):
                pe.wait_ge(S["smax_in"], k + 1)
                pe.transpose(bk[7][:, 0:P], mxa, ident[:, :]).then_inc(S["smax_turned"], 1)
                pe.wait_ge(S["smax_diag"], k + 1)
                pe.matmul(bk[7][:, P:2 * P], ones[:, :], diag, start=True, stop=True).then_inc(S["smax_bc"], 1)
                pe.wait_ge(S["smax_sum"], k + 1)
                pe.matmul(bk[7][:, 2 * P:3 * P], ones[:, :], mxa, start=True, stop=True).then_inc(S["smax_den"], 1)

            softmax(0)
            pe.wait_ge(S["newlog_read"], 1)
            for b in range(NB):
                arrived(pe, ("av", b))
                src = slot_of(("av", b))
                for c in range(DC):
                    for g in range(NG):
                        mm = pe.matmul(bk[6][:, (b * DC + c) * 2:(b * DC + c) * 2 + 2], src[:, g * D + c * P:g * D + (c + 1) * P],
                                       LA[:, b, g, 2 * c:2 * c + 2], start=(g == 0), stop=(g == NG - 1))
                mm.then_inc(S["pva_done"], 1)
            pe.wait_ge(S["smax_norm"], 1)
            pe.matmul(bk[7][:, 0:384], ones[0:NB, :], LA[0:NB, :, 3:6, :], start=True, stop=True).then_inc(S["pnew_done"], 1)

            def product(blk0, n_blk, e0, rhs):
                for j in range(n_blk):
                    blk = blk0 + j
                    pe.wait_ge(w_landed[blk % NW], 16 * (blk // NW + 1))
                    for half in range(2):
                        tile(blk, half, e0 + 2 * j + half, rhs).then_inc(S["gemm_done"], 1)

            def mlp(layer, blk_up, e_up, blk_dn, e_dn):
                pe.wait_ge(S["h_ready"], DC * (2 * layer + 2))
                with pe.Fori(0, 4) as it:
                    for j in range(4):
                        blk = blk_up + j
                        pe.wait_ge(w_landed[blk % NW], it * 16 + 16 * (blk // NW + 1))
                        for half in range(2):
                            pe.wait_ge(S["gemm_evac"], it * 8 + (e_up + 2 * j + half - 1))
                            for c in range(DC):
                                mm = pe.matmul(bk[half][:, 0:R], wring[:, blk % NW, c, half * P:(half + 1) * P], hT[:, c, :],
                                               start=(c == 0), stop=(c == DC - 1))
                            mm.then_inc(S["gemm_done"], 1)
                pe.wait_ge(S["up_ready"], 32 * (layer + 1))
                with pe.Fori(0, 4) as nb:
                    for kg in range(4):
                        blk = blk_dn + kg
                        pe.wait_ge(w_landed[blk % NW], nb * 16 + 16 * (blk // NW + 1))
                        for half in range(2):
                            if kg == 0:
                                pe.wait_ge(S["gemm_evac"], nb * 2 + (e_dn + half - 1))
                            for c in range(DC):
                                f = kg * DC + c
                                mm = pe.matmul(bk[half][:, 0:R], wring[:, blk % NW, c, half * P:(half + 1) * P], upT[:, f * R:(f + 1) * R],
                                               start=(f == 0), stop=(f == FC - 1))
                            mm.then_inc(S["gemm_done"], 1)

            pe.wait_ge(S["ot_evac"], DC)
            pe.wait_ge(S["oa_ready"], 2)
            product(B_AOUT, 4, E_AOUT, oT)
            norm(1)
            mlp(0, B_UP0, E_UP0, B_DN0, E_DN0)
            norm(2)

            pe.wait_ge(S["w1_in"], 48)
            pe.transpose(bk[0][:, 0:32], pe_row, ident[0:32, 0:32]).then_inc(S["pe_turned"], 1)
            pe.wait_ge(S["pe_ready"], 1)
            for k in range(2):
                for j in range(16):
                    mm = pe.matmul(bk[0][:, 64 + k:65 + k], w1[:, k, j // 8, j % 8, :], peT[:, k * 16 + j:k * 16 + j + 1],
                                   start=(j == 0), stop=(j == 15))
            mm.then_inc(S["peb_done"], 1)
            pe.wait_ge(S["peb_ready"], 1)
            turn(n_cmp0)

            def compressed(b):
                pe.wait_ge(S["hid_ready"], 2 * b + 2)
                if b:
                    pe.wait_ge(S["comp_read"], b)
                pe.matmul(bk[0][0:HD, 0:508], w2[:, 0, :], hid[:, 0, :], start=True, stop=True)
                for g in range(KVH):
                    mm = pe.matmul(bk[1][0:CMPS, g * HD:(g + 1) * HD], hid[:, 1, g * CMPS:(g + 1) * CMPS], w2[:, 1, :], start=True, stop=True)
                mm.then_inc(S["comp_done"], 1)

            for n in range(n_cmp0, n_sel0):
                if n + 1 < n_sel0:
                    turn(n + 1)
                it, _, (k, sp_) = groups[n]
                b, m = it[1], (n - n_cmp0) % 16
                sq = squares(n).rearrange("p (g n) -> p g n", g=KVH)
                if m == 0 and b >= 2:
                    pe.wait_ge(S["hid_ready"], 2 * (b - 1))
                acc = bk[4 + 2 * (b % 2) + k][:, 0:508]
                for i in range(2):
                    mm = pe.matmul(acc, w1[:, k, i, sp_, :], sq[:, :, i:i + CMPS], start=(sp_ == 0 and i == 0), stop=(sp_ == 7 and i == 1))
                mm.then_inc(S["sq_used"], 1)
                if m == 4 and b:
                    compressed(b - 1)
            compressed(NB - 1)
            pe.wait_ge(S["comp_read"], NB)

            pe.wait_ge(S["h_ready"], 3 * DC)
            held = None
            for j in range(11):
                blk = B_BIN + j
                pe.wait_ge(w_landed[blk % NW], 16 * (blk // NW + 1))
                for half in range(2 if j < 10 else 1):
                    i = 2 * j + half
                    tile(blk, half, E_BIN + i, hT, P if i < 20 else 48).then_inc(S["gemm_done"], 1 if i < 20 else 2)
                    if held is not None:
                        pe.wait_ge(S["gemm_evac"], E_BIN + held + 1)
                        rows(48 + held - 8, kvtmp[:, held % 2, :])
                    held = i if 8 <= i < 20 else None
            pe.wait_ge(S["gate_ready"], 1)
            pe.wait_ge(S["rows_evac"], 60)
            for rt in range(RT):
                mm = pe.transpose(bk[2][:, rt * 48:(rt + 1) * 48], gT[0:48, rt * P:(rt + 1) * P], ident[0:48, 0:48])
            mm.then_inc(S["gate_turned"], 1)
            pe.wait_ge(S["gate_diag"], 1)
            pe.matmul(bk[3][:, 0:384], ones[0:48, :], gdiag, start=True, stop=True).then_inc(S["gateb_done"], 1)
            pe.wait_ge(S["gates_ready"], 2)
            pe.wait_ge(S["gemm_evac"], E_BOUT)
            for k in range(2):
                for j in range(16):
                    mm = pe.matmul(bk[4 + k][:, 0:60], w1[:, k, j // 8, j % 8, :], XTp[:, k, j % 8, :, j // 8:j // 8 + CMP],
                                   start=(j == 0), stop=(j == 15))
            mm.then_inc(S["hidp_done"], 1)
            pe.wait_ge(S["hidp_ready"], 2)
            pe.matmul(bk[0][0:HD, 0:60], w2[:, 0, :], hidp[:, 0, :], start=True, stop=True)
            for g in range(KVH):
                mm = pe.matmul(bk[1][0:CMP, g * HD:(g + 1) * HD], hidp[:, 1, g * CMP:(g + 1) * CMP], w2[:, 1, :], start=True, stop=True)
            mm.then_inc(S["kcp_done"], 1)
            pe.wait_ge(S["kcp_ready"], 1)

            U0 = 2 * H

            def score_b(u):
                h, qt = u // 2, u % 2
                q0, c, g, n = HD * (h % 2), h // 2, h // KVH, (qt + 1) * P
                if u >= 2:
                    pe.wait_ge(S["logits_read"], U0 + u - 1)
                q = qT2[q0:q0 + HD, c, qt * P:(qt + 1) * P]
                b, o = (bk[0], 16) if qt == 0 else (bk[1], 0)
                pe.matmul((bk[0] if qt == 0 else bk[2])[:, 0:CMP], q, kcP[q0:q0 + HD, g * CMP:(g + 1) * CMP], start=True, stop=True)
                for k in range(2):
                    mm = pe.matmul(b[:, o + k * n:o + (k + 1) * n], q, kD[q0:q0 + HD, k, g, 0:n], start=True, stop=True)
                mm.then_inc(S["scores_done"], 1)

            def pv_b(u):
                h, qt = u // 2, u % 2
                g, n = h // KVH, qt + 1
                pe.wait_ge(S["pt_ready"], U0 + u + 1)
                if u >= 2:
                    pe.wait_ge(S["o_evac"], U0 + u - 1)
                o, pt = bk[6 + u % 2], PB[:, u % 2, :]
                pe.matmul(o[:, 0:HD], pt[0:CMP, 0:P], vcP[0:CMP, g * HD:(g + 1) * HD], start=True, stop=True)
                for k in range(2):
                    for j in range(n):
                        mm = pe.matmul(o[:, (k + 1) * HD:(k + 2) * HD], pt[:, (1 + k * n + j) * P:(2 + k * n + j) * P],
                                       kvrow[:, j, (3 + 2 * k) * GW + g * HD:(3 + 2 * k) * GW + (g + 1) * HD],
                                       start=(j == 0), stop=(j == n - 1))
                mm.then_inc(S["pv_done"], 1)

            pe.wait_ge(S["qb_ready"], 6)
            score_b(0)
            for u in range(2 * H):
                if u + 1 < 2 * H:
                    score_b(u + 1)
                n = 2 * (u % 2 + 1)
                turn_probs((U0 + u, u), [CMP + 1] + [P] * n, LB[:, u % 2, :])
                if u:
                    pv_b(u - 1)
            pv_b(2 * H - 1)
            pe.wait_ge(S["o_evac"], 4 * H)
            turn_out(DC)

            for k in range(2):
                for gp in range(2):
                    mm = pe.matmul(bk[6][0:NB, k * P + gp * 64:k * P + (gp + 1) * 64], kTn[:, k, gp, :], qb2[:, :, gp * 8:(gp + 1) * 8],
                                   start=True, stop=True)
            for b in range(NB):
                for g in range(KVH):
                    mm = pe.matmul(bk[6][0:CMPS, 256 + b * H + 4 * g:256 + b * H + 4 * g + 4], kcS[:, b, g * CMPS:(g + 1) * CMPS],
                                   q0[:, b, 4 * g:4 * g + 4], start=True, stop=True)
            mm.then_inc(S["newlog_done"], 1)
            softmax(1)
            pe.wait_ge(S["imp_ready"], 1)
            pe.matmul(bk[7][0:32, 384:384 + NBLK], impb, imp_w[:, :], start=True, stop=True).then_inc(S["score_done"], 1)
            turn(n_sel0)
            for n in range(n_sel0, n_groups):
                if n + 1 < n_groups:
                    turn(n + 1)
                it, _, (s,) = groups[n]
                i = NB + (it[1] if it[0] == "sk" else NB + it[1])
                sq = squares(n)
                if s == 0 and i >= NB + 2:
                    pe.wait_ge(S["qk_read"], i - 1)
                for j in range(4):
                    o = (s + j // 2) * H + (j % 2) * 8
                    mm = pe.matmul(bk[4 + i % 2][:, o:o + 8], sq[:, j * P:(j + 1) * P], qb2[:, it[1], (j % 2) * 8:(j % 2) * 8 + 8],
                                   start=True, stop=True)
                mm.then_inc(S["sq_used"], 1)
            pe.wait_ge(S["rank_ready"], 1)
            pe.transpose(bk[0][0:NBLK, 0:32], rank, ident[0:32, 0:32]).then_inc(S["rank_turned"], 1)
            pe.wait_ge(S["rankt_ready"], 1)
            pe.matmul(bk[0][:, 64:96], blk_e[:, :], rankT, start=True, stop=True).then_inc(S["selm_done"], 1)
            softmax(2)
            softmax(3)
            pe.wait_ge(S["smax_exp"], 4)
            pe.wait_ge(S["newlog_read"], 2)
            for b in range(NB):
                for g in range(2):
                    mm = pe.matmul(bk[6][:, b * H + 8 * g:b * H + 8 * g + 8], vcS[0:CMPS, b, g * P:(g + 1) * P],
                                   LC[0:CMPS, b, 0, 8 * g:8 * g + 8], start=True, stop=True)
            mm.then_inc(S["pvc_done"], 1)
            for k, (kind, ns, L) in enumerate((("sv", 16, LS), ("wv", 4, LSW))):
                for b in range(NB):
                    arrived(pe, (kind, b))
                    src = slot_of((kind, b))
                    for g in range(2):
                        o = (k + 1) * P + b * H + 8 * g
                        for s in range(ns):
                            pe.matmul(bk[6][:, o:o + 8], src[:, s * GW + g * P:s * GW + (g + 1) * P], L[:, b, s, 8 * g:8 * g + 8],
                                      start=(s == 0), stop=False)
                        v0 = (3 + 2 * k) * GW + g * P
                        mm = pe.matmul(bk[6][:, o:o + 8], kvnew[:, v0:v0 + P], L[0:NB, b, ns, 8 * g:8 * g + 8], start=False, stop=True)
                    mm.then_inc(S["pvs_done" if k == 0 else "pvw_done"], 1)

            pe.wait_ge(S["ot_evac"], 2 * DC)
            pe.wait_ge(S["ob_ready"], 2)
            product(B_BOUT, 4, E_BOUT, oT)
            norm(3)
            mlp(1, B_UP1, E_UP1, B_DN1, E_DN1)
            norm(4)
            pe.wait_ge(S["h_ready"], 5 * DC)
            for c in range(DC):
                rows(60 + c, hT[:, c, :])

        @block.vector
        def _(dve):
            own = [0]

            def link(ins):
                own[0] += 1
                ins.then_inc(S["dve_own"], 1)
                dve.wait_ge(S["dve_own"], own[0])

            for c in range(DC):
                dve.wait_ge(S["gemm_done"], c + 1)
                dve.tensor_copy(xT[:, c, :], bk[c % 2][:, 0:R]).then_inc(S["gemm_evac"], 1)
            dve.wait_ge(S["gains_turned"], 1)
            dve.tensor_copy(gains[:, :], bk[2][:, 0:40]).then_inc(S["gains_ready"], 1)

            def norm(n, e):
                dve.wait_ge(S["gemm_evac"], e)
                for c in range(DC):
                    dve.tensor_tensor(oT[:, c, :], xT[:, c, :], xT[:, c, :], ALU.mult).then_inc(S["sq_ready"], 1)
                dve.wait_ge(S["sumsq_done"], n + 1)
                dve.tensor_scalar(rv[:, 0, :], bk[7][:, 0:R], 1.0 / D, EPS, ALU.mult, ALU.add).then_inc(S["var_ready"], 1)
                dve.wait_ge(S["std_ready"], n + 1)
                y, s = rv[:, 1, :], rv[:, 2, :]
                link(dve.reciprocal(y, y))
                link(dve.tensor_tensor(s, y, y, ALU.mult))
                link(dve.tensor_tensor(s, s, rv[:, 0, :], ALU.mult))
                link(dve.tensor_scalar(s, s, -0.5, 1.5, ALU.mult, ALU.add))
                link(dve.tensor_tensor(y, y, s, ALU.mult))
                for c in range(DC):
                    dve.scalar_tensor_tensor(hT[:, c, :], xT[:, c, :], gains[:, n * DC + c:n * DC + c + 1] if n == 4 else
                                             gains[:, GAIN[n] + c:GAIN[n] + c + 1], y, ALU.mult, ALU.mult).then_inc(S["h_ready"], 1)

            GAIN = [0, 16, 8, 24, 32]
            norm(0, 8)
            for i in range(8):
                dve.wait_ge(S["bias_done"], i + 1)
                dve.tensor_copy(bias[:, :, 32 * i:32 * i + 32], bk[3 + i % 2].rearrange("p (k h) -> p h k", h=H)).then_inc(S["bias_evac"], 1)
            dve.wait_ge(S["bias_done"], 9)
            link(dve.tensor_tensor(bias_s[:, :, :], bk[5][:, 0:NSL * H].rearrange("p (s h) -> p s h", h=H),
                                   mslot[:, :].unsqueeze(2).broadcast_to([P, NSL, H]), ALU.add))
            dve.tensor_tensor(nbias[:, :, :], bias_s[0:NB, SL_NEW, :].unsqueeze(1).broadcast_to([NB, NB, H]),
                              mnew[:, :].unsqueeze(2).broadcast_to([NB, NB, H]), ALU.add).then_inc(S["bias_evac"], 1)
            dve.wait_ge(S["bias_done"], 10)
            for rt in range(RT):
                ins = dve.tensor_tensor(bias_c[:, rt, :, :], bk[6][:, rt * CMP * H:(rt + 1) * CMP * H].rearrange("p (n h) -> p h n", h=H),
                                        mcmp[:, rt, :].unsqueeze(1).broadcast_to([P, H, CMP]), ALU.add)
            ins.then_inc(S["bias_evac"], 1)

            n_rows = 0
            for i in range(72):
                g, kind, c = i // 24, i // 8 % 3, i % 8
                dve.wait_ge(S["gemm_done"], done_at(0) + i + 1)
                src = bk[i % 2][:, 0:R]
                if kind == 2:
                    if n_rows >= 2:
                        dve.wait_ge(S["rows_turned"], n_rows - 1)
                    dve.tensor_copy(vTn[:, g, c, :], src[:, SEQ:R])
                if kind:
                    n_rows += 1
                dve.tensor_copy((qT[:, g, c, :], kT[:, g, c, :], vtmp[:, i % 2, :])[kind], src).then_inc(S["gemm_evac"], 1)

            dve.wait_ge(S["gemm_evac"], E_AOUT)
            link(dve.memset(qbd.rearrange("p g b c e -> p (g b c e)"), 0.0))
            for e in range(2):
                for g in range(NG):
                    ins = dve.tensor_copy(qbd[64 * e:64 * e + 64, g, :, :, e], qT[64 * e:64 * e + 64, g, :, SEQ:R].rearrange("p c b -> p b c"))
                ins.then_inc(S["qbd_ready"], 1)

            def out_a(u):
                h, qt = u // 2, u % 2
                dve.wait_ge(S["pv_done"], u + 1)
                dve.wait_ge(S["probs_ready"], u + 1)
                link(dve.reciprocal(rc2[:, u % 4:u % 4 + 1], sm2[:, u % 4:u % 4 + 1]))
                dve.tensor_scalar(orow[:, qt, h * HD:(h + 1) * HD], bk[6 + u % 2][:, 0:HD], rc2[:, u % 4:u % 4 + 1], None, ALU.mult)\
                   .then_inc(S["o_evac"], 1)

            dve.wait_ge(S["rows_stored"], 16 * 12)
            for u in range(2 * H):
                h, qt = u // 2, u % 2
                dve.wait_ge(S["scores_done"], u + 1)
                dve.wait_ge(S["mix_ready"], h + 1)
                if u >= 2:
                    dve.wait_ge(S["probs_turned"], u - 1)
                L, mix = LG[:, u % 2, :], mixes[h % 2]
                bm = mix.rearrange("p (g k) -> p g k", g=NG)
                if qt == 0:
                    ins = dve.scalar_tensor_tensor(L[:, 0:384].rearrange("p (g k) -> p g k", g=NG), bk[0][:, 0:384].rearrange("p (g k) -> p g k", g=NG),
                                                   SCALE, bm[:, :, P:2 * P], ALU.mult, ALU.add)
                else:
                    dve.scalar_tensor_tensor(L[:, 0:512], bk[1][:, :], SCALE, mix[:, 0:512], ALU.mult, ALU.add)
                    ins = dve.scalar_tensor_tensor(L[:, 512:768], bk[2][:, 0:256], SCALE, mix[:, 512:768], ALU.mult, ALU.add)
                ins.then_inc(S["logits_read"], 1)
                dve.wait_ge(S["logits_read"], u + 1)
                dve.tensor_reduce(mx2[:, u % 4:u % 4 + 1], L[:, 0:384 * (qt + 1)], AX.X, ALU.max, negate=True).then_inc(S["max_ready"], 1)
                if u >= 2:
                    out_a(u - 2)
            out_a(2 * H - 2)
            out_a(2 * H - 1)

            def turn_out(first):
                for c in range(DC):
                    dve.wait_ge(S["ot_turned"], first + c + 1)
                    dve.tensor_copy(oT[:, c, 0:SEQ], bk[c % 2][:, 0:SEQ]).then_inc(S["ot_evac"], 1)

            turn_out(0)

            def square(n):
                dve.wait_ge(S["sq_turned"], n + 1)
                if n >= NT:
                    dve.wait_ge(S["sq_used"], n - NT + 1)
                copy_squares(dve.tensor_copy, n).then_inc(S["sq_evac_d"], 1)

            def soft1(k, L, nb_s):
                dve.tensor_reduce(mxa, L.rearrange("p b s h -> p b h s"), AX.X, ALU.max).then_inc(S["smax_in"], 1)
                dve.wait_ge(S["smax_turned"], k + 1)
                link(dve.tensor_reduce(m1, bk[7][:, 0:P], AX.X, ALU.max))
                dve.tensor_scalar(diag, ident[:, :], m1, None, ALU.mult).then_inc(S["smax_diag"], 1)
                dve.wait_ge(S["smax_bc"], k + 1)
                mb = bk[7][:, P:2 * P].rearrange("p (b h) -> p b h", h=H).unsqueeze(2).broadcast_to([P, NB, nb_s, H])
                dve.tensor_tensor(L, L, mb, ALU.subtract).then_inc(S["smax_sub"], 1)

            def soft2(k, L, slot):
                dve.wait_ge(S["smax_exp"], k + 1)
                dve.tensor_reduce(mxa, L.rearrange("p b s h -> p b h s"), AX.X, ALU.add).then_inc(S["smax_sum"], 1)
                dve.wait_ge(S["smax_den"], k + 1)
                dve.reciprocal(rs[:, slot, :], bk[7][:, 2 * P:3 * P]).then_inc(S["smax_norm"], 1)

            dve.wait_ge(S["pv_done"], 2 * H)
            link(dve.memset(LA.rearrange("p b s h -> p (b s h)"), NEG))
            dve.wait_ge(S["newlog_done"], 1)
            for g in range(NG):
                for b in range(NB):
                    v = bk[6][0:NB, g * P:(g + 1) * P].rearrange("p (c b e) -> p b c e", c=DC, b=NB)[:, b]
                    ins = dve.scalar_tensor_tensor(LA[0:NB, b, 3 + g, :].rearrange("p (c e) -> p c e", e=2), v, SCALE,
                                                   nbias[:, b, :].rearrange("p (c e) -> p c e", e=2), ALU.mult, ALU.add)
            ins.then_inc(S["newlog_read"], 1)
            for n in range(0, n_cmp0, 2):
                square(n)
                if n % 6 == 2 and n >= 6:
                    b = n // 6 - 1
                    dve.wait_ge(S["sq_used"], 6 * b + 6)
                    dve.scalar_tensor_tensor(LA[:, b, 0:3, :].rearrange("p s h -> p (s h)"), bk[4 + b % 2][:, 0:48], SCALE,
                                             bias_s[:, 0:3, :].rearrange("p s h -> p (s h)"), ALU.mult, ALU.add).then_inc(S["qk_read"], 1)
            dve.wait_ge(S["sq_used"], n_cmp0)
            dve.scalar_tensor_tensor(LA[:, NB - 1, 0:3, :].rearrange("p s h -> p (s h)"), bk[4 + (NB - 1) % 2][:, 0:48], SCALE,
                                     bias_s[:, 0:3, :].rearrange("p s h -> p (s h)"), ALU.mult, ALU.add).then_inc(S["qk_read"], 1)
            dve.wait_ge(S["qk_read"], NB)
            dve.wait_ge(S["newlog_read"], 1)
            soft1(0, LA, 6)
            soft2(0, LA, 0)
            dve.wait_ge(S["pnew_done"], 1)
            link(dve.tensor_copy(pn.rearrange("p b g c e -> p (b g c e)"), bk[7][:, 0:384]))
            for e in range(2):
                h0 = 64 * e
                for g in range(NG):
                    ins = dve.tensor_tensor(pv3[h0:h0 + 64, g], pn[h0:h0 + 64, :, g, :, e], vTn[h0:h0 + 64, g].rearrange("p c b -> p b c"), ALU.mult)
            link(ins)
            link(dve.tensor_reduce(pv1.rearrange("p b c -> p (b c)"), pv3.rearrange("p g b c -> p (b c) g"), AX.X, ALU.add))
            dve.wait_ge(S["pva_done"], NB)
            for e in range(2):
                h0 = 64 * e
                acc = bk[6][h0:h0 + 64, 0:P].rearrange("p (b c e) -> p b c e", b=NB, e=2)[:, :, :, e]
                ins = dve.tensor_tensor(pv1[h0:h0 + 64], pv1[h0:h0 + 64], acc, ALU.add)
            link(ins)
            dve.wait_ge(S["smax_norm"], 1)
            for e in range(2):
                h0 = 64 * e
                den = rs[h0:h0 + 64, 0, :].rearrange("p (b c e) -> p b c e", b=NB, e=2)[:, :, :, e]
                dve.tensor_tensor(oT[h0:h0 + 64, :, SEQ:R], pv1[h0:h0 + 64].rearrange("p b c -> p c b"), den.rearrange("p b c -> p c b"),
                                  ALU.mult).then_inc(S["oa_ready"], 1)

            def add_tiles(e0, blk0):
                for i in range(DC):
                    dve.wait_ge(S["gemm_done"], done_at(blk0) + i + 1)
                    dve.tensor_tensor(xT[:, i, :], bk[i % 2][:, 0:R], xT[:, i, :], ALU.add).then_inc(S["gemm_evac"], 1)

            x_flat = xT.rearrange("p c r -> p (c r)")

            def mlp(blk_up, e_up, blk_dn):
                with dve.Fori(0, 4) as it:
                    for j in range(8):
                        col = dve.snap((it * 8 + j) * R)
                        done = dve.snap(it * 8 + (done_at(blk_up) + j + 1))
                        evac = dve.snap(it * 8 + (e_up + j + 1))
                        dve.wait_ge(S["gemm_done"], done)
                        dve.tensor_scalar(up_all[:, bass.ds(col, R)], bk[j % 2][:, 0:R], 0.0, None, ALU.max).then_inc(S["gemm_evac"], 1)
                        dve.wait_ge(S["gemm_evac"], evac)
                        dve.tensor_tensor(up_all[:, bass.ds(col, R)], up_all[:, bass.ds(col, R)], up_all[:, bass.ds(col, R)], ALU.mult)\
                           .then_inc(S["up_ready"], 1)
                with dve.Fori(0, 4) as nb:
                    for half in range(2):
                        col = dve.snap((nb * 2 + half) * R)
                        done = dve.snap(nb * 8 + (done_at(blk_dn) + 6 + half + 1))
                        dve.wait_ge(S["gemm_done"], done)
                        dve.tensor_tensor(x_flat[:, bass.ds(col, R)], bk[half][:, 0:R], x_flat[:, bass.ds(col, R)], ALU.add)\
                           .then_inc(S["gemm_evac"], 1)

            add_tiles(E_AOUT, B_AOUT)
            norm(1, E_UP0)
            mlp(B_UP0, E_UP0, B_DN0)
            norm(2, E_BIN)

            dve.wait_ge(S["pe_turned"], 1)
            dve.tensor_copy(peT, bk[0][:, 0:32]).then_inc(S["pe_ready"], 1)
            dve.wait_ge(S["peb_done"], 1)
            dve.tensor_copy(peb, bk[0][:, 64:66]).then_inc(S["peb_ready"], 1)

            def compressed(b):
                dve.wait_ge(S["comp_done"], b + 1)
                dve.tensor_copy(kcS[:, b, :], bk[0][0:HD, 0:508])
                dve.tensor_copy(vcS[0:CMPS, b, :], bk[1][0:CMPS, 0:GW]).then_inc(S["comp_read"], 1)

            for n in range(n_cmp0, n_sel0, 2):
                square(n)
                m = n - n_cmp0
                if m % 16 == 8 and m >= 16:
                    compressed(m // 16 - 1)
            compressed(NB - 1)

            for i in range(21):
                dve.wait_ge(S["gemm_done"], done_at(B_BIN) + i + 1 + (i == 20))
                src = bk[i % 2][:, 0:R]
                if i < 8:
                    ins = dve.tensor_copy(qT2[:, i, :], src)
                elif i < 20:
                    j = i - 8
                    if j >= 2:
                        dve.wait_ge(S["rows_turned"], 48 + j - 1)
                    kind = j // 2
                    if kind in (2, 4):
                        dve.tensor_copy(kTn[:, kind // 2 - 1, j % 2, :], src[:, SEQ:R])
                    for y in range(2 if kind in (0, 1, 2, 4) else 0):
                        for x in range(2):
                            g, half = 2 * (j % 2) + x, src[64 * x:64 * x + 64, 0:SEQ]
                            if kind < 2:
                                dve.tensor_copy(XTp[64 * y:64 * y + 64, kind, :, g, :], half.rearrange("p (n s e) -> p s n e", s=8, e=2)[:, :, :, y])
                            else:
                                dve.tensor_copy(kD[64 * y:64 * y + 64, kind // 2 - 1, g, :], half)
                    ins = dve.tensor_copy(kvtmp[:, i % 2, :], src)
                else:
                    ins = dve.tensor_copy(gT[0:48], bk[0][0:48, 0:R])
                ins.then_inc(S["gemm_evac"], 1)
            dve.wait_ge(S["gate_turned"], 1)
            dve.tensor_copy(grow.rearrange("p t h k -> p t (h k)"), bk[2][:, 0:96].rearrange("p (t n) -> p t n", t=RT)).then_inc(S["gates_ready"], 1)
            dve.wait_ge(S["rows_turned"], 60)
            dve.tensor_tensor(gdiag.rearrange("p (j b) -> p j b", j=48), ident[0:48, 0:48].unsqueeze(2).broadcast_to([48, 48, NB]),
                              gT[0:48, SEQ:R].unsqueeze(1).broadcast_to([48, 48, NB]), ALU.mult).then_inc(S["gate_diag"], 1)
            dve.wait_ge(S["gateb_done"], 1)
            dve.tensor_copy(gB.rearrange("p h k b -> p (h k b)"), bk[3][:, 0:384]).then_inc(S["gates_ready"], 1)
            link(dve.memset(qb2.rearrange("p b h -> p (b h)"), 0.0))
            for e in range(2):
                q = qT2[64 * e:64 * e + 64, :, SEQ:R].rearrange("p c b -> p b c")
                dve.tensor_copy(q0.rearrange("p b (c e) -> p b c e", e=2)[:, :, :, e], q).then_inc(S["qb_ready"], 1)
                for x in range(2):
                    for gp in range(2):
                        c = 4 * gp + 2 * x
                        ins = dve.tensor_copy(qb2[64 * x:64 * x + 64].rearrange("p b (c e) -> p b c e", e=2)[:, :, c:c + 2, e], q[:, :, c:c + 2])
                    ins.then_inc(S["qb_ready"], 1)
            dve.wait_ge(S["kcp_done"], 1)
            for y in range(2):
                dve.tensor_copy(kcP[64 * y:64 * y + 64], bk[0][0:HD, 0:60])
            dve.tensor_copy(vcP[0:CMP, :], bk[1][0:CMP, 0:GW]).then_inc(S["kcp_ready"], 1)

            U0 = 2 * H

            def out_b(u):
                h, qt = u // 2, u % 2
                dve.wait_ge(S["pv_done"], U0 + u + 1)
                dve.wait_ge(S["probs_ready"], U0 + u + 1)
                sm, rc = sm2[:, 3 * (u % 4):3 * (u % 4) + 3], rc2[:, 3 * (u % 4):3 * (u % 4) + 3]
                link(dve.tensor_scalar(rc, sm, 1e-30, None, ALU.max))
                link(dve.reciprocal(rc, rc))
                link(dve.tensor_tensor(rc, rc, grow[:, qt, h, :], ALU.mult))
                o, b = orow[:, qt, h * HD:(h + 1) * HD], bk[6 + u % 2]
                link(dve.tensor_tensor(ob3, b[:, 0:3 * HD].rearrange("p (k d) -> p k d", k=3), rc.unsqueeze(2).broadcast_to([P, 3, HD]), ALU.mult))
                dve.tensor_reduce(o, ob3.rearrange("p k d -> p d k"), AX.X, ALU.add).then_inc(S["o_evac"], 1)

            dve.wait_ge(S["kcp_done"], 1)
            link(dve.memset(LB.rearrange("p i n -> p (i n)"), NEG))
            dve.wait_ge(S["mix_ready"], H + 1)
            for u in range(2 * H):
                h, qt = u // 2, u % 2
                n = (qt + 1) * P
                dve.wait_ge(S["scores_done"], U0 + u + 1)
                if u >= 2:
                    dve.wait_ge(S["probs_turned"], U0 + u - 1)
                L = LB[:, u % 2, :]
                dve.scalar_tensor_tensor(L[:, 0:CMP], (bk[0] if qt == 0 else bk[2])[:, 0:CMP], SCALE, bias_c[:, qt, h, :], ALU.mult, ALU.add)
                b, o = (bk[0], 16) if qt == 0 else (bk[1], 0)
                bm = bias[:, h, 256 - n:256].unsqueeze(1).broadcast_to([P, 2, n])
                L2 = L[:, 16:16 + 2 * n].rearrange("p (k n) -> p k n", k=2)
                dve.scalar_tensor_tensor(L2, b[:, o:o + 2 * n].rearrange("p (k n) -> p k n", k=2), SCALE, bm, ALU.mult, ALU.add).then_inc(S["logits_read"], 1)
                dve.wait_ge(S["logits_read"], U0 + u + 1)
                mx = mx2[:, 3 * (u % 4):3 * (u % 4) + 3]
                dve.tensor_reduce(mx[:, 0:1], L[:, 0:CMP], AX.X, ALU.max, negate=True)
                link(dve.tensor_reduce(mx[:, 1:3], L2, AX.X, ALU.max, negate=True))
                dve.tensor_scalar(mx[:, 0:1], mx[:, 0:1], 1e29, None, ALU.min).then_inc(S["max_ready"], 1)
                if u >= 2:
                    out_b(u - 2)
            out_b(2 * H - 2)
            out_b(2 * H - 1)
            turn_out(DC)

            link(dve.memset(LS[:, :, 16, :], NEG))
            link(dve.memset(LSW[:, :, 4, :], NEG))
            link(dve.memset(LC.rearrange("p b s h -> p (b s h)"), NEG))
            dve.wait_ge(S["newlog_done"], 2)
            for b in range(NB):
                for k, L, s in ((0, LS, 16), (1, LSW, 4)):
                    v = bk[6][0:NB, k * P:(k + 1) * P].rearrange("p (g b x) -> p b g x", g=2, b=NB)[:, b]
                    dve.scalar_tensor_tensor(L[0:NB, b, s, :].rearrange("p (g x) -> p g x", g=2), v, SCALE,
                                             nbias[:, b, :].rearrange("p (g x) -> p g x", g=2), ALU.mult, ALU.add)
            dve.scalar_tensor_tensor(LC[0:CMPS, :, 0, :], bk[6][0:CMPS, 256:384].rearrange("p (b h) -> p b h", b=NB), SCALE,
                                     bias_s[0:CMPS, SL_CMP, :].unsqueeze(1).broadcast_to([CMPS, NB, H]), ALU.mult, ALU.add).then_inc(S["newlog_read"], 1)
            dve.wait_ge(S["newlog_read"], 2)
            soft1(1, LC, 1)
            soft2(1, LC, 0)
            dve.wait_ge(S["smax_norm"], 2)
            link(dve.tensor_tensor(mxa, LC.rearrange("p b s h -> p (b s h)"), rs[:, 0, :], ALU.mult))
            dve.tensor_reduce(impb, mxa.rearrange("p (n r) -> p n r", r=4), AX.X, ALU.add).then_inc(S["imp_ready"], 1)
            dve.wait_ge(S["score_done"], 1)
            link(dve.tensor_copy(score, bk[7][0:32, 384:384 + NBLK]))
            dve.memset(score[:, 0:1], 1e4)
            link(dve.memset(score[:, NBLK - 2:NBLK], 1e4))
            s_i = score.unsqueeze(1).broadcast_to([32, NBLK, NBLK])
            s_j = score.unsqueeze(2).broadcast_to([32, NBLK, NBLK])
            dve.tensor_tensor(rk[0], s_i, s_j, ALU.is_ge)
            link(dve.tensor_tensor(rk[1], s_i, s_j, ALU.is_gt))
            link(dve.tensor_tensor(rk[0], rk[0], rk[1], ALU.subtract))
            dve.wait_ge(S["new_stored"], 16)
            link(dve.tensor_tensor(rk[0], rk[0], before, ALU.mult))
            link(dve.tensor_tensor(rk[0], rk[0], rk[1], ALU.add))
            link(dve.tensor_reduce(rank, rk[0], AX.X, ALU.add))
            dve.tensor_scalar(rank, rank, TOPK - 0.5, NEG, ALU.is_gt, ALU.mult).then_inc(S["rank_ready"], 1)

            def logits_b(i):
                b, sel = i % NB, i < NB
                dve.wait_ge(S["sq_used"], n_sel0 + (8 * (i + 1) if sel else 64 + 2 * (i - NB + 1)))
                L, n, s0 = (LS, 16, SL_SEL) if sel else (LSW, 4, SL_WIN)
                dve.scalar_tensor_tensor(L[:, b, 0:n, :].rearrange("p s h -> p (s h)"), bk[4 + i % 2][:, 0:n * H], SCALE,
                                         bias_s[:, s0:s0 + n, :].rearrange("p s h -> p (s h)"), ALU.mult, ALU.add).then_inc(S["qk_read"], 1)

            made = 0
            for n in range(n_sel0, n_groups, 2):
                square(n)
                m = n - n_sel0
                full = m // 8 if m <= 64 else 8 + (m - 64) // 2
                while made < min(full, 2 * NB):
                    if m <= 64 and m % 8 < 2 and m != 64:
                        break
                    logits_b(made)
                    made += 1
            while made < 2 * NB:
                logits_b(made)
                made += 1
            dve.wait_ge(S["rank_turned"], 1)
            dve.tensor_copy(rankT, bk[0][0:NBLK, 0:32]).then_inc(S["rankt_ready"], 1)
            dve.wait_ge(S["selm_done"], 1)
            link(dve.tensor_copy(selm.rearrange("p b g -> p (b g)"), bk[0][:, 64:96]))
            dve.wait_ge(S["qk_read"], 3 * NB)
            for b in range(NB):
                v = LS[:, b, 0:16, :].rearrange("p s (g r) -> p s g r", g=KVH)
                ins = dve.tensor_tensor(v, v, selm[:, b].unsqueeze(1).unsqueeze(3).broadcast_to([P, 16, KVH, 4]), ALU.add)
            link(ins)
            soft1(2, LS, 17)
            soft2(2, LS, 1)
            soft1(3, LSW, 5)
            soft2(3, LSW, 2)
            dve.wait_ge(S["smax_norm"], 4)
            for k in range(3):
                v = rs[:, k, :].rearrange("p (b h) -> p b h", b=NB)
                ins = dve.tensor_tensor(v, v, gB[:, :, k, :].rearrange("p h b -> p b h"), ALU.mult)
            link(ins)
            dve.wait_ge(S["pvc_done"], 1)
            dve.wait_ge(S["pvs_done"], NB)
            dve.wait_ge(S["pvw_done"], NB)
            link(dve.tensor_tensor(ob, bk[6][:, 0:384].rearrange("p (k n) -> p k n", k=3), rs[:, :, :], ALU.mult))
            link(dve.tensor_tensor(ob[:, 0], ob[:, 0], ob[:, 1], ALU.add))
            link(dve.tensor_tensor(ob[:, 0], ob[:, 0], ob[:, 2], ALU.add))
            for e in range(2):
                for x in range(2):
                    for gp in range(2):
                        c = 4 * gp + 2 * x
                        ins = dve.tensor_copy(oT[64 * e:64 * e + 64, c:c + 2, SEQ:R],
                                              ob[64 * x:64 * x + 64, 0].rearrange("p (b c e) -> p c b e", b=NB, e=2)[:, c:c + 2, :, e])
                ins.then_inc(S["ob_ready"], 1)

            add_tiles(E_BOUT, B_BOUT)
            norm(3, E_UP1)
            mlp(B_UP1, E_UP1, B_DN1)
            norm(4, E_ALL)

        @block.scalar
        def _(act):
            def norm(n):
                act.wait_ge(S["var_ready"], n + 1)
                nc.scalar.activation(rv[:, 1, :], rv[:, 0, :], ACT.Sqrt).then_inc(S["std_ready"], 1)

            norm(0)

            for r in range(48):
                g, kv, c = r // 16, r // 8 % 2, r % 8
                if c == 0 and r:
                    act.wait_ge(S["rows_stored"], 32 * (r // 8))
                act.wait_ge(S["rows_turned"], r + 1)
                b = bk[2 + r % 2]
                dst = krow[:, :, c * P:(c + 1) * P] if kv == 0 else V[:, :, g, c * P:(c + 1) * P]
                nc.scalar.copy(dst, b[:, 0:SEQ].rearrange("p (t n) -> p t n", t=RT))
                nc.scalar.copy(rown[:, c * P:(c + 1) * P], b[0:NB, SEQ:SEQ + P]).then_inc(S["rows_evac"], 1)
                if c == DC - 1:
                    act.wait_ge(S["rows_evac"], r + 1)
                    out = t[f"a_win{g}_prompt"][0, 0].rearrange("(t p) a h d -> p t a (h d)", p=P)[:, :, kv, :]
                    src = krow if kv == 0 else V[:, :, g, :]
                    n_t = out.shape[1]
                    act.dma_start(out, src[:, RT - n_t:RT, :]).then_inc(S["rows_stored"], 16)
                    act.dma_start(t[f"a_win{g}_sample"][0, :, DIL[g][0] - 1, kv].rearrange("b h d -> b (h d)"), rown).then_inc(S["rows_stored"], 16)

            def copy_pt(u, parts_cols, PTb):
                act.wait_ge(S["probs_turned"], u + 1)
                if u >= 2:
                    act.wait_ge(S["pv_done"], u - 1)
                for parts, bank, c0, n, o in parts_cols:
                    ins = nc.scalar.copy(PTb[0:parts, o:o + n], bk[bank][0:parts, c0:c0 + n])
                ins.then_inc(S["pt_ready"], 1)

            def pt_a(u):
                copy_pt(u, [(P, 3, 0, 384, 0)] if u % 2 == 0 else [(P, 4, 0, 512, 0), (P, 5, 0, 256, 512)], PT[:, u % 2, :])

            for u in range(2 * H):
                act.wait_ge(S["max_ready"], u + 1)
                if u >= 4:
                    act.wait_ge(S["o_evac"], u - 3)
                n = 384 * (u % 2 + 1)
                L = LG[:, u % 2, 0:n]
                nc.scalar.activation(L, L, ACT.Exp, bias=mx2[:, u % 4:u % 4 + 1], accum_out=sm2[:, u % 4:u % 4 + 1]).then_inc(S["probs_ready"], 1)
                if u:
                    pt_a(u - 1)
            pt_a(2 * H - 1)

            def square(n):
                act.wait_ge(S["sq_turned"], n + 1)
                if n >= NT:
                    act.wait_ge(S["sq_used"], n - NT + 1)
                copy_squares(nc.scalar.copy, n).then_inc(S["sq_evac_a"], 1)

            def softmax(k, L):
                act.wait_ge(S["smax_sub"], k + 1)
                nc.scalar.activation(L, L, ACT.Exp).then_inc(S["smax_exp"], 1)

            for n in range(1, n_cmp0, 2):
                square(n)
            softmax(0, LA)
            norm(1)

            act.wait_ge(S["oa_ready"], 2)
            act.dma_start(w1.rearrange("p k i s n -> p (k i s) n"), t["b_phi_w1"][0].rearrange("k (j p) n -> p (k j) n", p=P)).then_inc(S["w1_in"], 16)
            act.dma_start(w2, t["b_phi_w2"][0].rearrange("k p d -> p k d")).then_inc(S["w1_in"], 16)
            act.dma_start(pe_row, t["b_phi_pe"][0].rearrange("k (j s) d -> (k j) (s d)", s=2)).then_inc(S["w1_in"], 16)
            norm(2)
            act.wait_ge(S["peb_ready"], 1)

            def hidden(b):
                act.wait_ge(S["sq_used"], n_cmp0 + 16 * (b + 1))
                if b:
                    act.wait_ge(S["comp_done"], b)
                for k in range(2):
                    nc.scalar.activation(hid[:, k, :], bk[4 + 2 * (b % 2) + k][:, 0:508], ACT.Relu, bias=peb[:, k:k + 1]).then_inc(S["hid_ready"], 1)

            for n in range(n_cmp0 + 1, n_sel0, 2):
                square(n)
                m = n - n_cmp0
                if m % 16 == 3 and m > 16:
                    hidden(m // 16 - 1)
            hidden(NB - 1)

            for j in range(12):
                r = 48 + j
                act.wait_ge(S["rows_turned"], r + 1)
                b = bk[2 + r % 2]
                nc.scalar.copy(kvrow[:, :, j * P:(j + 1) * P], b[:, 0:SEQ].rearrange("p (t n) -> p t n", t=RT))
                nc.scalar.copy(kvnew[:, j * P:(j + 1) * P], b[0:NB, SEQ:SEQ + P]).then_inc(S["rows_evac"], 1)
            act.wait_ge(S["gemm_evac"], E_BOUT)
            nc.scalar.activation(gT[0:48], gT[0:48], ACT.Sigmoid).then_inc(S["gate_ready"], 1)
            act.wait_ge(S["rows_evac"], 60)
            act.dma_start(t["b_kv_prompt"][0, 0].rearrange("(t p) k g d -> p t (k g d)", p=P), kvrow[:, :, 0:4 * GW]).then_inc(S["rows_stored"], 16)
            act.dma_start(t["b_win_prompt"][0, 0].rearrange("(t p) k g d -> p t (k g d)", p=P), kvrow[:, :, 4 * GW:6 * GW]).then_inc(S["rows_stored"], 16)
            act.dma_start(t["b_kv_sample"][0].rearrange("b a k g d -> (b a) (k g d)"), kvnew[:, 0:4 * GW]).then_inc(S["rows_stored"], 16)
            act.dma_start(t["b_win_sample"][0, :, 511].rearrange("b k g d -> b (k g d)"), kvnew[:, 4 * GW:6 * GW]).then_inc(S["rows_stored"], 16)
            act.wait_ge(S["hidp_done"], 1)
            for k in range(2):
                nc.scalar.activation(hidp[:, k, :], bk[4 + k][:, 0:60], ACT.Relu, bias=peb[:, k:k + 1]).then_inc(S["hidp_ready"], 1)

            U0 = 2 * H

            def pt_b(u):
                parts = ([(CMP + 1, 3, 0, P, 0), (P, 3, P, 256, P)] if u % 2 == 0 else
                         [(CMP + 1, 4, 0, P, 0), (P, 4, P, 384, P), (P, 5, 0, P, 512)])
                act.wait_ge(S["probs_turned"], U0 + u + 1)
                if u >= 2:
                    act.wait_ge(S["pv_done"], U0 + u - 1)
                for np_, bank, c0, n, o in parts:
                    ins = nc.scalar.copy(PB[0:np_, u % 2, o:o + n], bk[bank][0:np_, c0:c0 + n])
                ins.then_inc(S["pt_ready"], 1)

            for u in range(2 * H):
                act.wait_ge(S["max_ready"], U0 + u + 1)
                if u >= 4:
                    act.wait_ge(S["o_evac"], U0 + u - 3)
                n = (u % 2 + 1) * P
                L, o = LB[:, u % 2, :], 3 * (u % 4)
                for k, (a, w) in enumerate(((0, CMP), (16, n), (16 + n, n))):
                    ins = nc.scalar.activation(L[:, a:a + w], L[:, a:a + w], ACT.Exp, bias=mx2[:, o + k:o + k + 1], accum_out=sm2[:, o + k:o + k + 1])
                ins.then_inc(S["probs_ready"], 1)
                if u:
                    pt_b(u - 1)
            pt_b(2 * H - 1)
            act.wait_ge(S["pv_done"], 4 * H)
            act.wait_ge(S["qb_ready"], 6)
            act.wait_ge(S["rows_stored"], 16 * 16)
            act.dma_start(before.rearrange("p j i -> p (j i)"), t["c_before"]).then_inc(S["new_stored"], 16)
            softmax(1, LC)
            for n in range(n_sel0 + 1, n_groups, 2):
                square(n)
            softmax(2, LS)
            softmax(3, LSW)
            norm(3)
            norm(4)
            y = wring.rearrange("p i c n -> p (i c n)")[:, 0:3 * D].rearrange("p (t n) -> p t n", t=3)
            for c in range(DC):
                r = 60 + c
                act.wait_ge(S["rows_turned"], r + 1)
                b = bk[2 + r % 2]
                nc.scalar.copy(y[:, 0:2, c * P:(c + 1) * P], b[:, 0:SEQ].rearrange("p (t n) -> p t n", t=RT))
                nc.scalar.copy(y[0:NB, 2, c * P:(c + 1) * P], b[0:NB, SEQ:SEQ + P]).then_inc(S["rows_evac"], 1)
            act.wait_ge(S["rows_evac"], 68)
            act.dma_start(t["y_prompt"].rearrange("a (t p) n -> p (a t) n", p=P), y[:, 0:2, :]).then_inc(S["rows_stored"], 16)
            act.dma_start(t["y_sample"].rearrange("b a n -> (b a) n"), y[0:NB, 2, :]).then_inc(S["rows_stored"], 16)
            act.wait_ge(S["rows_stored"], 16 * 18)


OUTS = [("y_prompt", (1, SEQ, D)), ("y_sample", (NB, 1, D)),
        ("a_win0_prompt", (1, 1, 128, 2, H, HD)), ("a_win0_sample", (1, NB, 128, 2, H, HD)),
        ("a_win1_prompt", (1, 1, SEQ, 2, H, HD)), ("a_win1_sample", (1, NB, 512, 2, H, HD)),
        ("a_win2_prompt", (1, 1, SEQ, 2, H, HD)), ("a_win2_sample", (1, NB, 2048, 2, H, HD)),
        ("b_kv_prompt", (1, 1, SEQ, 4, KVH, HD)), ("b_kv_sample", (1, NB, 1, 4, KVH, HD)),
        ("b_win_prompt", (1, 1, SEQ, 2, KVH, HD)), ("b_win_sample", (1, NB, 512, 2, KVH, HD))]


def kernel(**inputs):
    import numpy as _np
    import concourse.bacc as _bacc
    from concourse.bass_utils import run_bass_kernel_spmd as _run

    nc = _bacc.Bacc("TRN2", target_bir_lowering=False, num_devices=1)
    arrays = {n: _np.ascontiguousarray(a) for n, a in inputs.items()}
    arrays.update(constants())
    t = {n: nc.dram_tensor(n, a.shape, mybir.dt.from_np(a.dtype), kind="ExternalInput").ap() for n, a in arrays.items()}
    for n, shape in OUTS:
        t[n] = nc.dram_tensor(n, shape, F32, kind="ExternalOutput").ap()
    program(nc, t)
    r = _run(nc, [arrays], core_ids=[0])
    return tuple(r.results[0][n] for n, _ in OUTS)
```
